# Optimizing a Trainium2 kernel written in Bass

```python
import math
import jax, jax.numpy as jnp
from jax import lax
import numpy as np

D_MODEL = 2048
BATCH = 1
SEQ = 256
DEPTH = 1
DEC_BATCH = 8
DEC_SEQ = 8
PAST_LEN = 2048
PAGE_SIZE = 128

GLA_HEADS = 4
GLA_DK = D_MODEL // 2 // GLA_HEADS
GLA_DV = D_MODEL // GLA_HEADS
GLA_GATE_RANK = 16
GLA_GATE_NORM = 16.0
HG_EXPAND = 128
HG_HEADS = D_MODEL // HG_EXPAND
HG_DK = HG_EXPAND
HG_DV = D_MODEL // HG_HEADS
D_FF = 4 * D_MODEL
CHUNK = 64
EPS = 1e-6

IN_SPLITS = (
    GLA_HEADS * GLA_DK,
    GLA_HEADS * GLA_DK,
    GLA_HEADS * GLA_DV,
    GLA_GATE_RANK,
    GLA_HEADS * GLA_DV,
    HG_HEADS * HG_DK,
    HG_HEADS * HG_DK,
    HG_HEADS * HG_DV,
    HG_HEADS * HG_DV,
    D_MODEL,
    D_MODEL,
)
D_IN = sum(IN_SPLITS)

kernel_name = "gla_hgrn2_gated_merge_step"

def _rmsnorm(x, g):
    xf = x.astype(jnp.float32)
    xf = xf * lax.rsqrt(jnp.mean(xf * xf, axis=-1, keepdims=True) + EPS)
    return (xf * g.astype(jnp.float32)).astype(x.dtype)

def _chunked_gated_linear_attention(q, k, v, log_g, s0):
    B, L, H, dk = q.shape
    dv = v.shape[-1]
    c = math.gcd(L, CHUNK)
    n = L // c

    def to_chunks(t):
        return t.astype(jnp.float32).reshape(B, n, c, H, t.shape[-1]).transpose(1, 0, 3, 2, 4)

    mask = jnp.tril(jnp.ones((c, c), dtype=bool))[None, None, :, :, None]

    def step(s, inp):
        qc, kc, vc, gc = inp
        a = jnp.cumsum(gc, axis=2)
        o_inter = jnp.einsum('bhtk,bhkv->bhtv', qc * jnp.exp(a), s)
        diff = a[:, :, :, None, :] - a[:, :, None, :, :]
        decay = jnp.exp(jnp.where(mask, diff, -jnp.inf))
        scores = jnp.einsum('bhtk,bhsk,bhtsk->bhts', qc, kc, decay)
        o = o_inter + jnp.einsum('bhts,bhsv->bhtv', scores, vc)
        a_last = a[:, :, -1:, :]
        s_new = s * jnp.exp(a_last[:, :, 0, :, None]) + jnp.einsum(
            'bhsk,bhsv->bhkv', kc * jnp.exp(a_last - a), vc)
        return s_new, o

    s_fin, o = lax.scan(step, s0.astype(jnp.float32),
                        (to_chunks(q), to_chunks(k), to_chunks(v), to_chunks(log_g)))
    o = o.transpose(1, 0, 3, 2, 4).reshape(B, L, H, dv)
    return o, s_fin

def _layer(x, s_gla, s_hg, lb, norm_mix, w_in, w_gate2, b_gate2, gla_norm, hg_norm,
           w_branch_a, w_branch_b, w_out, norm_mlp, w_up, w_down):
    B, L, _ = x.shape
    h = _rmsnorm(x, norm_mix)
    proj = h @ w_in
    idx = list(np.cumsum(IN_SPLITS)[:-1])
    q_a, k_a, v_a, gr_a, r_a, q_b, f_b, i_b, r_b, m_a, m_b = jnp.split(proj, idx, axis=-1)

    qa = q_a.reshape(B, L, GLA_HEADS, GLA_DK) * (GLA_DK ** -0.5)
    ka = k_a.reshape(B, L, GLA_HEADS, GLA_DK)
    va = v_a.reshape(B, L, GLA_HEADS, GLA_DV)
    log_ga = jax.nn.log_sigmoid((gr_a @ w_gate2 + b_gate2).astype(jnp.float32)) / GLA_GATE_NORM
    log_ga = log_ga.reshape(B, L, GLA_HEADS, GLA_DK)
    o_a, s_a = _chunked_gated_linear_attention(qa, ka, va, log_ga, s_gla)
    o_a = _rmsnorm(o_a, gla_norm).reshape(B, L, GLA_HEADS * GLA_DV).astype(x.dtype) * jax.nn.silu(r_a)

    f = lb + (1.0 - lb) * jax.nn.sigmoid(f_b.astype(jnp.float32))
    log_f = jnp.log(f).reshape(B, L, HG_HEADS, HG_DK)
    kb = (1.0 - f).reshape(B, L, HG_HEADS, HG_DK)
    qb = jax.nn.silu(q_b).reshape(B, L, HG_HEADS, HG_DK)
    ib = i_b.reshape(B, L, HG_HEADS, HG_DV)
    o_b, s_b = _chunked_gated_linear_attention(qb, kb, ib, log_f, s_hg)
    o_b = _rmsnorm(o_b, hg_norm).reshape(B, L, HG_HEADS * HG_DV).astype(x.dtype) * jax.nn.silu(r_b)

    merged = jax.nn.sigmoid(m_a) * (o_a @ w_branch_a) + jax.nn.sigmoid(m_b) * (o_b @ w_branch_b)
    x = x + merged @ w_out

    hid = jnp.square(jax.nn.relu(_rmsnorm(x, norm_mlp) @ w_up))
    x = x + hid @ w_down
    return x, s_a.astype(x.dtype), s_b.astype(x.dtype)

def setup_inputs(seed: int = 0) -> dict:
    key = jax.random.key(seed)
    ks = jax.random.split(key, 20)

    def nrm(k, shape, scale):
        return jax.random.normal(k, shape, jnp.float32) * scale

    return {
        "x_prompt": nrm(ks[0], (BATCH, SEQ, D_MODEL), 1.0),
        "x_sample": nrm(ks[1], (DEC_BATCH, DEC_SEQ, D_MODEL), 1.0),
        "state_gla": nrm(ks[2], (DEPTH, DEC_BATCH, GLA_HEADS, GLA_DK, GLA_DV), 0.5),
        "state_hgrn": nrm(ks[3], (DEPTH, DEC_BATCH, HG_HEADS, HG_DK, HG_DV), 0.5),
        "norm_mix": 1.0 + nrm(ks[4], (DEPTH, D_MODEL), 0.02),
        "w_in": nrm(ks[5], (DEPTH, D_MODEL, D_IN), D_MODEL ** -0.5),
        "w_gate2": nrm(ks[6], (DEPTH, GLA_GATE_RANK, GLA_HEADS * GLA_DK), GLA_GATE_RANK ** -0.5),
        "b_gate2": nrm(ks[7], (DEPTH, GLA_HEADS * GLA_DK), 0.1),
        "gla_norm": 1.0 + nrm(ks[8], (DEPTH, GLA_DV), 0.02),
        "hg_norm": 1.0 + nrm(ks[9], (DEPTH, HG_DV), 0.02),
        "hg_lower_bound": nrm(ks[10], (DEPTH + 1, HG_HEADS * HG_DK), 0.5),
        "w_branch_a": nrm(ks[11], (DEPTH, GLA_HEADS * GLA_DV, D_MODEL), (GLA_HEADS * GLA_DV) ** -0.5),
        "w_branch_b": nrm(ks[12], (DEPTH, HG_HEADS * HG_DV, D_MODEL), (HG_HEADS * HG_DV) ** -0.5),
        "w_out": nrm(ks[13], (DEPTH, D_MODEL, D_MODEL), D_MODEL ** -0.5),
        "norm_mlp": 1.0 + nrm(ks[14], (DEPTH, D_MODEL), 0.02),
        "w_up": nrm(ks[15], (DEPTH, D_MODEL, D_FF), D_MODEL ** -0.5),
        "w_down": nrm(ks[16], (DEPTH, D_FF, D_MODEL), D_FF ** -0.5),
        "norm_final": 1.0 + nrm(ks[17], (D_MODEL,), 0.02),
    }

def reference(x_prompt, x_sample, state_gla, state_hgrn, norm_mix, w_in, w_gate2, b_gate2,
              gla_norm, hg_norm, hg_lower_bound, w_branch_a, w_branch_b, w_out, norm_mlp,
              w_up, w_down, norm_final):
    lower_bounds = jnp.cumsum(jax.nn.softmax(hg_lower_bound.astype(jnp.float32), axis=0), axis=0)

    xp, xs = x_prompt, x_sample
    gla_p, hg_p, gla_s, hg_s = [], [], [], []
    for l in range(DEPTH):
        params = (lower_bounds[l], norm_mix[l], w_in[l], w_gate2[l], b_gate2[l], gla_norm[l],
                  hg_norm[l], w_branch_a[l], w_branch_b[l], w_out[l], norm_mlp[l], w_up[l], w_down[l])
        zero_gla = jnp.zeros((BATCH, GLA_HEADS, GLA_DK, GLA_DV), jnp.float32)
        zero_hg = jnp.zeros((BATCH, HG_HEADS, HG_DK, HG_DV), jnp.float32)
        xp, sa_p, sb_p = _layer(xp, zero_gla, zero_hg, *params)
        xs, sa_s, sb_s = _layer(xs, state_gla[l], state_hgrn[l], *params)
        gla_p.append(sa_p); hg_p.append(sb_p); gla_s.append(sa_s); hg_s.append(sb_s)

    y_prompt = _rmsnorm(xp, norm_final)
    y_sample = _rmsnorm(xs, norm_final)
    new_gla_prompt = jnp.stack(gla_p, axis=0)
    new_hgrn_prompt = jnp.stack(hg_p, axis=0)
    new_gla_sample = jnp.stack(gla_s, axis=0)
    new_hgrn_sample = jnp.stack(hg_s, axis=0)
    return (y_prompt, y_sample, new_gla_prompt, new_hgrn_prompt, new_gla_sample, new_hgrn_sample)


_drawn_inputs = setup_inputs


def setup_inputs(seed=0):
    import zlib

    import numpy as np

    out = dict(_drawn_inputs(seed))
    spreads = {}
    factors = {'gla_norm': 8.0, 'hg_norm': 7.925, 'norm_mlp': 3.232, 'norm_final': 2.817}
    for name, (base, spread) in spreads.items():
        noise = np.random.default_rng([zlib.crc32(name.encode()), seed]).standard_normal(out[name].shape)
        drawn = base * np.exp(spread * noise) if base else spread * noise
        out[name] = __import__('jax').numpy.asarray(drawn.astype(out[name].dtype))
    for name, factor in factors.items():
        out[name] = (out[name] * factor).astype(out[name].dtype)
    return out
```

```python
from contextlib import ExitStack, contextmanager

import concourse.bass as bass
from concourse import mybir

ALU = mybir.AluOpType
ACT = mybir.ActivationFunctionType
F32 = mybir.dt.float32
F32R = mybir.dt.float32r
U8 = mybir.dt.uint8

P = 128
D = 2048
KT = D // P
NPR = 256
SB, SL = 8, 8
NSM = SB * SL
T = NPR + NSM
HA, DKA, DVA = 4, 256, 512
HB = 16
HPAIRS = HB // 2
RANK = 16
FF = 4 * D
EPS = 1e-6
GATE_NORM = 16.0
W2 = 256
NS2 = D // W2
UNITS = 4
UK = KT // UNITS
QUARTERS = FF // D
SCRATCH = 9836
SCRATCH = 9836
SCRATCH = 9836
SCRATCH = 9836
LEVELS = 8

C_QA, C_KA, C_VA, C_GR = 0, 1024, 2048, 4096
C_RA = C_GR + RANK
C_QB, C_FB, C_IB, C_RB, C_MA, C_MB = (C_RA + D * (1 + n) for n in range(6))

M_GLA, M_MA = 0, 3 * HA
M_HG = M_MA + NS2
M_MB = M_HG + 2 * HPAIRS
M_OUT = M_MB + NS2
M_UP = M_OUT + NS2 // 2
M_DOWN = M_UP + NS2 // 2
M_Q = NS2

V_MIX, V_MLP, V_FIN, V_LB0, V_LB1, V_BG, V_GA, V_GB = 0, 16, 32, 48, 64, 80, 88, 92
V_N = 93

GLA, HG = 0, 1
FILLS0 = (1, 0, 0, 0)
FILLS = ((10, 4, 13, 13), (7, 5, 5, 5))


def per(phase, n, gla, hg, k):
    return n * gla + k if phase == GLA else n * hg + (HA * gla + k)


def fills(bank, phase, n, k):
    return per(phase, n, FILLS[0][bank], FILLS[1][bank], k + FILLS0[bank])


def wait_from(eng, sem, value):
    if not isinstance(value, int) or value > 0:
        eng.wait_ge(sem, value)


class Tally:

    def __init__(self, eng, sem):
        self.eng, self.sem, self.before, self.here = eng, sem, 0, 0

    def link(self, ins, wait=None):
        ins.then_inc(self.sem, 1)
        self.here += 1
        if wait is None:
            self.eng.wait_ge(self.sem, self.before + self.here)
        else:
            wait(self.eng, self.sem, self.before + self.here)

    @contextmanager
    def loop(self, first, last, each):
        before, here = self.before, self.here
        with self.eng.Fori(first, last) as i:
            self.before, self.here = (i - first) * each + (before + here), 0
            yield i
        assert self.here == each, f"{self.here} links in a turn, not {each}"
        self.before, self.here = before, here + (last - first) * each


def gated_merge_step(nc, x_t, state_gla, state_hgrn, vectors, w_in, w_gate2, w_branch_a, w_branch_b, w_out,
                     w_up, w_down, ones_in, eye_in, own_in, masks_in,
                     y_t, gla_prompt, hgrn_prompt, gla_sample, hgrn_sample):
    ctx = ExitStack()
    with ctx:
        def sb(name, shape, dt=F32):
            return ctx.enter_context(nc.sbuf_tensor(name, shape, dt))

        def sem(name):
            return ctx.enter_context(nc.semaphore(name))

        raw = sb("raw", [P, 4, 2 * UK, W2])
        w_hi = sb("w_hi", [P, UNITS, UK, W2], F32R)
        w_lo = sb("w_lo", [P, UNITS, UK, W2], F32R)
        a_hi = sb("a_hi", [P, KT, T], F32R)
        a_lo = sb("a_lo", [P, KT, T], F32R)
        b_hi = sb("b_hi", [P, KT, T], F32R)
        b_lo = sb("b_lo", [P, KT, T], F32R)
        m_sb = sb("m_sb", [P, KT, T])
        s_sb = sb("s_sb", [P, SCRATCH])
        ones = sb("ones", [P, P])
        eye = sb("eye", [P, P])
        own = sb("own", [NSM, SB])
        masks = sb("masks", [P, P + 6 * 64], U8)
        vec = sb("vec", [P, V_N])
        lb = sb("lb", [P, KT])
        one_lb = sb("one_lb", [P, KT])
        soft = sb("soft", [P, 3, KT])
        gr = sb("gr", [RANK, T])
        wg = sb("wg", [RANK, DKA])

        AT_Q = 2 * T
        AT_K = AT_Q + 2 * T
        AT_G = AT_K + 2 * T
        AT_TOT = AT_G + 2 * T
        AT_V = AT_TOT + 2 * 310
        AT_SC = AT_V + 2 * T
        AT_U = AT_SC + 2 * 448
        AT_PS = AT_U + 4096
        AT_KTOK = AT_PS + 2 * P
        assert AT_KTOK + 3 * DKA == SCRATCH == AT_U + KT * T

        AT_Q = 2 * T
        AT_K = AT_Q + 2 * T
        AT_G = AT_K + 2 * T
        AT_TOT = AT_G + 2 * T
        AT_V = AT_TOT + 2 * 310
        AT_SC = AT_V + 2 * T
        AT_U = AT_SC + 2 * 448
        AT_PS = AT_U + 4096
        AT_KTOK = AT_PS + 2 * P
        assert AT_KTOK + 3 * DKA == SCRATCH == AT_U + KT * T

        AT_Q = 2 * T
        AT_K = AT_Q + 2 * T
        AT_G = AT_K + 2 * T
        AT_TOT = AT_G + 2 * T
        AT_V = AT_TOT + 2 * 310
        AT_SC = AT_V + 2 * T
        AT_U = AT_SC + 2 * 448
        AT_PS = AT_U + 4096
        AT_KTOK = AT_PS + 2 * P
        assert AT_KTOK + 3 * DKA == SCRATCH == AT_U + KT * T

        AT_Q = 2 * T
        AT_K = AT_Q + 2 * T
        AT_G = AT_K + 2 * T
        AT_TOT = AT_G + 2 * T
        AT_V = AT_TOT + 2 * 310
        AT_SC = AT_V + 2 * T
        AT_U = AT_SC + 2 * 448
        AT_PS = AT_U + 4096
        AT_KTOK = AT_PS + 2 * P
        assert AT_KTOK + 3 * DKA == SCRATCH == AT_U + KT * T

        def part(at, *shape):
            size = 1
            for x in shape:
                size *= x
            v = s_sb[:, at:at + size]
            if len(shape) == 2:
                v = v.rearrange("p (a b) -> p a b", b=shape[1])
            if len(shape) == 3:
                v = v.rearrange("p (a b c) -> p a b c", b=shape[1], c=shape[2])
            return v

        q_raw = part(0, 2, T)
        q = part(AT_Q, 2, T)
        k = part(AT_K, 2, T)
        g = part(AT_G, 2, T)
        tots = part(AT_TOT, 2, 310)
        v_t = part(AT_V, 2, T)
        sc = part(AT_SC, 2, 448)
        v_tok = [part(AT_U, 3, DVA), part(AT_U, 3, 256)]
        o_sb = [part(AT_U + 1536, 4, T), part(AT_U + 768, 2, T)]
        r_sb = [part(AT_U + 2816, 4, T), part(AT_U + 1408, 2, T)]
        st_hg = part(AT_U + 2048, 2, SB, P)
        ps_hg = part(AT_PS, 2, P)
        k_tok = part(AT_KTOK, 3, 256)
        x_res = part(AT_U, KT, T)
        k_own = part(0, 2, 512)
        sq = [part(0, 4, T), part(0, 2, T)]
        norm = v_t
        gate = k
        sq_sum, sq_new = part(0, 2, T), part(AT_Q, 2, T)
        hid_t, hid_f = k, g
        sq_in = part(0, 8, T)
        masks_f = part(AT_U, P + 6 * 64)
        m_flat = m_sb[:, :, :].rearrange("p a b -> p (a b)")
        st_gla = [m_flat[:, n * 1024:(n + 1) * 1024].rearrange("p (j v) -> p j v", j=2) for n in range(4)]
        ps_gla = m_flat[:, 4096:5120].rearrange("p (j v) -> p j v", j=2)

        TOT_AT = (None, 0, 160, 240, 280, 296, 304, 308)
        TOT_N = (T, 160, 80, 40, 16, 8, 4, 2)

        def tot(level):
            return g if level == 0 else tots[:, :, TOT_AT[level]:TOT_AT[level] + TOT_N[level]]

        def halves(v, level):
            if len(v.shape) == 3:
                return v.rearrange("p j (n h b) -> p j n h b", h=2, b=1 << level)
            return v.rearrange("p (n h b) -> p n h b", h=2, b=1 << level)

        def own_tot(j, b):
            at = TOT_AT[3] + NPR // SL + b
            return tots[:, j, at:at + 1]

        acc = [ctx.enter_context(nc.psum_tensor(f"acc{n}", [P, 2, 512], F32)) for n in range(2)]
        spare = [ctx.enter_context(nc.psum_tensor(f"spare{n}", [P, 512], F32)) for n in range(4)]

        consts_in = sem("consts_in")
        x_in = [sem(f"x_in{n}") for n in range(4)]
        x_res_in = sem("x_res_in")
        wg_in = sem("wg_in")
        raw_in = [sem(f"raw_in{n}") for n in range(4)]
        hi_made = sem("hi_made")
        lo_made = sem("lo_made")
        mm_done = sem("mm_done")
        acc_free = [sem(f"acc_free{n}") for n in range(2)]
        full = [sem(f"full{n}") for n in range(4)]
        free = [sem(f"free{n}") for n in range(4)]
        act_self = sem("act_self")
        dve_self = sem("dve_self")
        sq_in_made = sem("sq_in_made")
        sq_in_read = sem("sq_in_read")
        root_made = sem("root_made")
        h_made = sem("h_made")
        h_hi = sem("h_hi")
        h_ready = sem("h_ready")
        lb_max = sem("lb_max")
        lb_exp = sem("lb_exp")
        soft_made = sem("soft_made")
        log_made = sem("log_made")
        g_made = sem("g_made")
        sig_made = sem("sig_made")
        level_ready = sem("level_ready")
        k_final = sem("k_final")
        k_own_made = sem("k_own_made")
        sq_made = sem("sq_made")
        on_made = sem("on_made")
        on_hi = sem("on_hi")
        heads_ready = sem("heads_ready")
        st_in = [sem(f"st_in{n}") for n in range(4)]
        st_out = [sem(f"st_out{n}") for n in range(4)]
        ps_out = sem("ps_out")
        merged = sem("merged")
        merged_hi = sem("merged_hi")
        merged_ready = sem("merged_ready")
        res_sq = sem("res_sq")
        sq_summed = sem("sq_summed")
        res_hi = sem("res_hi")
        res_ready = sem("res_ready")
        hid_hi = sem("hid_hi")
        hid_ready = sem("hid_ready")
        y_made = sem("y_made")
        y_out = sem("y_out")
        went_on = {eng.engine: sem(f"went_on_{n}") for n, eng in
                   enumerate((nc.sync, nc.gpsimd, nc.scalar, nc.vector))}

        LATE = fills(0, HG, HPAIRS, 0)

        block = ctx.enter_context(nc.Block())

        def was_read(eng, bank, phase, n, fill, apart=False):
            if apart:
                wait_apart(eng, free[bank], fills(bank, phase, n, fill) + 1)
            else:
                eng.wait_ge(free[bank], fills(bank, phase, n, fill) + 1)

        def slab_done(eng, m, par):
            eng.wait_ge(mm_done, 8 * m + (4 * par + 4))

        def slab_read(eng, m, par):
            eng.wait_ge(acc_free[par], m + 1)

        def wait_apart(eng, sem, value):
            eng.wait_ge(sem, value)
            if not isinstance(value, int):
                eng.sem_inc(went_on[eng.engine], 1)

        def level_bank(phase, level):
            bank, fill = ((0, 0), (2, 0), (3, 0), (0, 1), (1, 1), (0, 2), (1, 2), (0, 3))[level]
            return bank, fill + (1 if phase == GLA and bank == 0 else 0)

        V_FILL, K_FILL = (1, 1), (3, 2)

        def score_fill(phase, n):
            bank, fill = level_bank(phase, LEVELS - 1)
            return bank, phase, n, fill

        def after(m, par):
            return (m, 1) if par == 0 else (m + 1, 0)

        @block.sync
        def _(sp):
            sp.dma_start(ones[:], ones_in).then_inc(consts_in, 16)
            sp.dma_start(vec[:], vectors).then_inc(consts_in, 16)
            x_tiles = x_t.rearrange("(k p) t -> p k t", p=P)
            for c in range(4):
                sp.dma_start(m_sb[:, 4 * c:4 * c + 4, :], x_tiles[:, 4 * c:4 * c + 4, :]).then_inc(x_in[c], 16)

            def slab(m, par, weights, row, col):
                for half in range(2):
                    slot = 2 * par + half
                    if not isinstance(m, int) or m >= 1:
                        wait_apart(sp, lo_made, 8 * m + (4 * par + 2 * half + 2 - 8))
                    src = weights[bass.ds(row + half * (D // 2), D // 2), bass.ds(col, W2)]
                    sp.dma_start(raw[:, slot, :, :], src.rearrange("(k p) n -> p k n", p=P))\
                      .then_inc(raw_in[slot], 16)

            def gla_weights(h):
                m = M_GLA + 3 * h
                slab(m, 1, w_in, 0, C_KA + DKA * h)
                slab(m + 1, 0, w_in, 0, C_QA + DKA * h)
                slab(m + 1, 1, w_in, 0, C_VA + DVA * h)
                slab(m + 2, 0, w_in, 0, C_VA + W2 + DVA * h)
                slab(m + 2, 1, w_in, 0, C_RA + DVA * h)
                slab(m + 3, 0, w_in, 0, C_RA + W2 + DVA * h)

            slab(0, 0, w_in, 0, C_GR)
            sp.dma_start(eye[:], eye_in).then_inc(consts_in, 16)
            sp.dma_start(own[:], own_in).then_inc(consts_in, 16)
            sp.dma_start(masks_f, masks_in).then_inc(consts_in, 16)
            gla_weights(0)
            with sp.Fori(1, HA) as h:
                gla_weights(h)
            with sp.Fori(0, NS2) as n:
                slab(M_MA + n, 1, w_in, 0, C_MA + W2 * n)
                slab(M_MA + n + 1, 0, w_branch_a, 0, W2 * n)
            with sp.Fori(0, HPAIRS) as n:
                slab(M_HG + 2 * n, 1, w_in, 0, C_FB + W2 * n)
                slab(M_HG + 2 * n + 1, 0, w_in, 0, C_QB + W2 * n)
                slab(M_HG + 2 * n + 1, 1, w_in, 0, C_IB + W2 * n)
                slab(M_HG + 2 * n + 2, 0, w_in, 0, C_RB + W2 * n)
            with sp.Fori(0, NS2) as n:
                slab(M_MB + n, 1, w_in, 0, C_MB + W2 * n)
                slab(M_MB + n + 1, 0, w_branch_b, 0, W2 * n)
            with sp.Fori(0, NS2 // 2) as n:
                slab(M_OUT + n, 1, w_out, 0, 2 * W2 * n)
                slab(M_OUT + n + 1, 0, w_out, 0, 2 * W2 * n + W2)
            with sp.Fori(0, QUARTERS) as c:
                with sp.Fori(0, NS2 // 2) as n:
                    slab(M_UP + M_Q * c + n, 1, w_up, 0, 2 * W2 * n + D * c)
                    slab(M_UP + M_Q * c + n + 1, 0, w_up, 0, 2 * W2 * n + D * c + W2)
                with sp.Fori(0, NS2 // 2) as n:
                    slab(M_DOWN + M_Q * c + n, 1, w_down, D * c, 2 * W2 * n)
                    slab(M_DOWN + M_Q * c + n + 1, 0, w_down, D * c, 2 * W2 * n + W2)
            y_tiles = y_t.rearrange("(k p) t -> p k t", p=P)
            for c in range(KT // 2):
                sp.wait_ge(y_made, c + 1)
                sp.dma_start(y_tiles[:, 2 * c:2 * c + 2, :], m_sb[:, 2 * c:2 * c + 2, :]).then_inc(y_out, 16)
            sp.wait_ge(y_out, 16 * (KT // 2))

        @block.gpsimd
        def _(pool):
            def own_rows(dst, src, b):
                return pool.tensor_scalar(dst, src, own[:, b:b + 1], 1.0, ALU.mult, ALU.mult)

            def gla_states(h):
                if not isinstance(h, int) or h > 0:
                    wait_apart(pool, full[1], fills(1, GLA, h, 0))
                pool.dma_start(wg[:], w_gate2[:, bass.ds(DKA * h, DKA)]).then_inc(wg_in, 16)

                def load(b):
                    if not isinstance(h, int) or 2 * h + b // 4 > 0:
                        wait_apart(pool, st_out[b % 4], 16 * (2 * h + b // 4))
                    src = state_gla[b, bass.ds(h, 1)].rearrange("h (j p) v -> p (h j) v", p=P)
                    pool.dma_start(st_gla[b % 4], src).then_inc(st_in[b % 4], 16)

                def rows(b):
                    if b >= 2:
                        wait_apart(pool, full[3], fills(3, GLA, h, 4 + b - 2) + 1)
                    own_rows(k_own[0:NSM, b % 2, 0:DKA], k_tok[0:NSM, 2, :], b).then_inc(k_own_made, 1)

                for b in range(4):
                    load(b)
                was_read(pool, 3, GLA, h, K_FILL[GLA], apart=True)
                rows(0)
                rows(1)
                for b in range(SB):
                    was_read(pool, 3, GLA, h, 4 + b, apart=True)
                    dst = gla_sample[b, bass.ds(h, 1)].rearrange("h (j p) v -> p (h j) v", p=P)
                    pool.dma_start(dst, st_gla[b % 4]).then_inc(st_out[b % 4], 16)
                    if b + 2 < SB:
                        rows(b + 2)
                    if 4 <= b + 3 < SB:
                        load(b + 3)
                was_read(pool, 3, GLA, h, 12, apart=True)
                dst = gla_prompt[bass.ds(h, 1)].rearrange("h (j p) v -> p (h j) v", p=P)
                pool.dma_start(dst, ps_gla).then_inc(ps_out, 16)

            def hgrn_states(n, first):
                if first:
                    pool.wait_ge(heads_ready, HA)
                for j in range(2):
                    wait_apart(pool, st_out[j], 16 * per(HG, n, 2, 1, 0))
                    src = state_hgrn[:, bass.ds(2 * n + j, 1)].rearrange("b h k v -> k (b h) v")
                    pool.dma_start(st_hg[:, j], src).then_inc(st_in[j], 16)
                was_read(pool, 3, HG, n, K_FILL[HG], apart=True)
                wait_apart(pool, full[3], fills(3, HG, n, 3) + 1)
                for c in range(4):
                    if c >= 2:
                        wait_apart(pool, full[c], fills(c, HG, n, 4) + 1)
                    for b in range(4):
                        ins = own_rows(k_own[0:NSM, c % 2, b * P:(b + 1) * P],
                                       k_tok[0:NSM, 2, (c // 2) * P:(c // 2 + 1) * P], 4 * (c % 2) + b)
                    ins.then_inc(k_own_made, 1)
                was_read(pool, 0, HG, n, 5, apart=True)
                pool.dma_start(hgrn_prompt[bass.ds(2 * n, 2)].rearrange("h k v -> k h v"), ps_hg)\
                    .then_inc(ps_out, 16)
                for j in range(2):
                    was_read(pool, (3, 1)[j], HG, n, 4, apart=True)
                    dst = hgrn_sample[:, bass.ds(2 * n + j, 1)].rearrange("b h k v -> k (b h) v")
                    pool.dma_start(dst, st_hg[:, j]).then_inc(st_out[j], 16)

            pool.wait_ge(consts_in, 16 * 5)
            pool.wait_ge(h_ready, 4)
            gla_states(0)
            with pool.Fori(1, HA) as h:
                gla_states(h)
            hgrn_states(0, True)
            with pool.Fori(1, HPAIRS) as n:
                hgrn_states(n, False)
            pool.wait_ge(heads_ready, HA + HPAIRS)
            for j in range(2):
                pool.wait_ge(st_out[j], 16 * per(HG, HPAIRS, 2, 1, 0))
            for j in range(2, 4):
                pool.wait_ge(st_out[j], 16 * 2 * HA)
            pool.wait_ge(ps_out, 16 * (HA + HPAIRS))
            pool.dma_start(x_res, x_t.rearrange("(k p) t -> p k t", p=P)).then_inc(x_res_in, 16)

        @block.tensor
        def _(pe):
            def unit(m, par, u, hi, lo, blocks=2):
                pe.wait_ge(lo_made, 8 * m + (4 * par + u + 1))
                if u == 0:
                    wait_from(pe, acc_free[par], m)
                for j in range(blocks):
                    for i in range(UK):
                        kt, cols = u * UK + i, slice(j * P, (j + 1) * P)
                        start, stop = kt == 0, kt == KT - 1
                        sums = acc[par][:, j, 0:T]
                        pe.matmul(sums, w_hi[:, u, i, cols], hi[:, kt, :], start=start, stop=False)
                        pe.matmul(sums, w_hi[:, u, i, cols], lo[:, kt, :], start=False, stop=False)
                        ins = pe.matmul(sums, w_lo[:, u, i, cols], hi[:, kt, :], start=False, stop=stop)
                ins.then_inc(mm_done, 1)

            def empty(bank, phase, n, fill):
                wait_from(pe, free[bank], fills(bank, phase, n, fill))

            def small(out, lhs, rhs, start=True, stop=True):
                return pe.matmul(out, lhs, rhs, start=start, stop=stop, skip_group_check=True)

            def scores(phase, n, level):
                pe.wait_ge(level_ready, per(phase, n, LEVELS, LEVELS, level + 1))
                first_bank, fill = level_bank(phase, level)
                heads = 2 if phase == HG else 1
                if level == 0:
                    for h in range(heads):
                        empty(h, phase, n, fill)
                else:
                    empty(first_bank, phase, n, fill)
                for h in range(heads):
                    keys = [h] if phase == HG else [0, 1]
                    bank = spare[h] if level == 0 else spare[first_bank]
                    at = NPR + NSM if level == 0 else 160 * h
                    todo = []
                    if level == 0:
                        todo += [(P, slice(tt * P, (tt + 1) * P), slice(tt * P, (tt + 1) * P), None, tt * P)
                                 for tt in range(2)]
                        todo += [(NSM, slice(NPR, T), slice(NPR, T), None, NPR)]
                    if level < 6:
                        todo += [(P, slice(tt * P, (tt + 1) * P), slice(tt * P, (tt + 1) * P), level, at + 64 * tt)
                                 for tt in range(2)]
                        if level < 3:
                            todo += [(NSM, slice(NPR, T), slice(NPR, T), level, at + P)]
                    elif level == 6:
                        todo += [(64, slice(tt * P, tt * P + 64), slice(tt * P + 64, tt * P + P), None, at + 64 * tt)
                                 for tt in range(2)]
                    else:
                        todo += [(P, slice(0, P), slice(P, NPR), None, at)]
                    for rows, s_at, t_at, lv, col in todo:
                        for j in keys:
                            qs = q[:, j, t_at] if lv is not None or level > 0 else q_raw[:, j, t_at]
                            if lv is not None:
                                qs = halves(qs, lv)[:, :, 1, :]
                            size = (t_at.stop - t_at.start) // (2 if lv is not None else 1)
                            ins = small(bank[0:rows, col:col + size], k[:, j, s_at], qs,
                                        j == keys[0], j == keys[-1])
                    if h == 0 and heads == 2 and level == 0:
                        ins.then_inc(full[0], 1)
                ins.then_inc(full[1 if phase == HG and level == 0 else first_bank], 1)

            def turn(src, phase, n, fill):
                for j in range(2):
                    empty(2 + j, phase, n, fill)
                    for tt, size in enumerate((P, P, NSM)):
                        ins = pe.transpose(spare[2 + j][0:size, tt * P:(tt + 1) * P],
                                           src[:, j, tt * P:tt * P + size], eye[:])
                    ins.then_inc(full[2 + j], 1)

            def gla_gate(h):
                pe.wait_ge(wg_in, 16 * (h + 1))
                for j in range(2):
                    empty(j, GLA, h, 0)
                    small(spare[j][:, 0:T], wg[:, j * P:(j + 1) * P], gr[:]).then_inc(full[j], 1)

            def gla_turn_v(h, c):
                slab_read(pe, M_GLA + 3 * h + 1 + c, 1 - c)
                turn(v_t, GLA, h, V_FILL[GLA] + c)

            def gla_turn_k(h):
                pe.wait_ge(k_final, h + 1)
                turn(k, GLA, h, K_FILL[GLA])

            def gla_sample_scores(h):
                was_read(pe, 3, GLA, h, V_FILL[GLA] + 1)
                was_read(pe, *score_fill(GLA, h))
                empty(1, GLA, h, 3)
                for v in range(4):
                    small(spare[1][:, v * NSM:(v + 1) * NSM], v_tok[GLA][0:NSM, 2, v * P:(v + 1) * P],
                          sc[0:NSM, 0, 384:448], v == 0, False)

            def gla_state(h, b):
                pe.wait_ge(st_in[b % 4], 32 * h + 16 * (b // 4 + 1))
                for v in range(4):
                    for j in range(2):
                        at = v * NSM + b * SL
                        ins = small(spare[1][:, at:at + SL], st_gla[b % 4][:, j, v * P:(v + 1) * P],
                                    q[:, j, NPR + b * SL:NPR + (b + 1) * SL], False, b == SB - 1 and j == 1)
                if b == SB - 1:
                    ins.then_inc(full[1], 1)
                pe.wait_ge(k_own_made, per(GLA, h, 8, 4, b + 1))
                for j in range(2):
                    empty(2 + j, GLA, h, 4 + b)
                    small(spare[2 + j][:, :], k_own[0:NSM, b % 2, j * P:(j + 1) * P],
                          v_tok[GLA][0:NSM, 2, :]).then_inc(full[2 + j], 1)

            def prompt_out(out, phase, h, v):
                cols = slice(v * P, (v + 1) * P)
                small(out[:, 0:NPR], v_tok[phase][:, 0, cols], sc[:, h, 0:NPR], True, False)
                return small(out[:, P:NPR], v_tok[phase][:, 1, cols], sc[:, h, NPR:NPR + P], False, True)

            def gla_prompt_out(h, v):
                empty(0, GLA, h, 5 + v)
                prompt_out(spare[0], GLA, 0, v).then_inc(full[0], 1)

            def gla_squares(h):
                pe.wait_ge(sq_made, h + 1)
                empty(0, GLA, h, 9)
                for v in range(4):
                    ins = small(spare[0][:, 0:T], ones[:], sq[GLA][:, v, :], v == 0, v == 3)
                ins.then_inc(full[0], 1)

            def gla_prompt_state(h):
                for j in range(2):
                    empty(2 + j, GLA, h, 12)
                    for tt in range(2):
                        ins = small(spare[2 + j][:, :], k_tok[:, tt, j * P:(j + 1) * P], v_tok[GLA][:, tt, :],
                                    tt == 0, tt == 1)
                    ins.then_inc(full[2 + j], 1)

            def gla_tail(h, slot):
                if slot < 3:
                    gla_state(h, 5 + slot)
                elif slot == 3:
                    gla_squares(h)
                else:
                    gla_prompt_state(h)

            def gla_head(h, tail):
                m = M_GLA + 3 * h
                for u in range(UNITS):
                    unit(m, 1, u, a_hi, a_lo)
                    if tail:
                        gla_tail(h - 1, u)
                for u in range(UNITS):
                    unit(m + 1, 0, u, a_hi, a_lo)
                    if tail and u == 0:
                        gla_tail(h - 1, 4)
                    if u == 1:
                        gla_gate(h)
                for u in range(UNITS):
                    unit(m + 1, 1, u, a_hi, a_lo)
                    if u > 0:
                        scores(GLA, h, u - 1)
                for u in range(UNITS):
                    unit(m + 2, 0, u, a_hi, a_lo)
                    scores(GLA, h, 3 + u)
                    if u == 2:
                        gla_turn_v(h, 0)
                for u in range(UNITS):
                    unit(m + 2, 1, u, a_hi, a_lo)
                    if u == 0:
                        scores(GLA, h, 7)
                    if u == 1:
                        gla_turn_v(h, 1)
                    if u == 2:
                        gla_turn_k(h)
                    if u == 3:
                        gla_sample_scores(h)
                        gla_state(h, 0)
                for u in range(UNITS):
                    unit(m + 3, 0, u, a_hi, a_lo)
                    gla_prompt_out(h, u)
                    gla_state(h, 1 + u)

            def hgrn_out(n):
                was_read(pe, 3, HG, n, V_FILL[HG])
                was_read(pe, *score_fill(HG, n))
                for j in range(2):
                    pe.wait_ge(st_in[j], 16 * per(HG, n, 2, 1, 1))
                    empty(j, HG, n, 4 - j)
                    out = spare[j]
                    prompt_out(out, HG, j, j)
                    small(out[:, NPR:T], v_tok[HG][0:NSM, 2, j * P:(j + 1) * P], sc[0:NSM, j, 384:448], False, False)
                    for b in range(SB):
                        at = slice(NPR + b * SL, NPR + (b + 1) * SL)
                        ins = small(out[:, at], st_hg[:, j, b, :], q[:, j, at], False, b == SB - 1)
                    ins.then_inc(full[j], 1)

            def hgrn_squares(n):
                for j in range(2):
                    was_read(pe, j, HG, n, 4 - j)
                    empty(2 + j, HG, n, 3)
                    small(spare[2 + j][:, 0:T], ones[:], sq[HG][:, j, :]).then_inc(full[2 + j], 1)

            def hgrn_prompt_states(n):
                empty(0, HG, n, 5)
                for j in range(2):
                    for tt in range(2):
                        cols = slice(j * P, (j + 1) * P)
                        ins = small(spare[0][:, cols], k_tok[:, tt, cols], v_tok[HG][:, tt, cols], tt == 0, tt == 1)
                ins.then_inc(full[0], 1)

            def hgrn_states(n, j):
                for half in range(2):
                    bank, fill = ((2 + half, 4), (half, (6, 4)[half]))[j]
                    pe.wait_ge(k_own_made, per(HG, n, 8, 4, 2 * j + half + 1))
                    empty(bank, HG, n, fill)
                    for b in range(4):
                        ins = small(spare[bank][:, b * P:(b + 1) * P], k_own[0:NSM, half, b * P:(b + 1) * P],
                                    v_tok[HG][0:NSM, 2, j * P:(j + 1) * P])
                    ins.then_inc(full[bank], 1)

            def hgrn_tail(n, slot):
                if slot == 0:
                    scores(HG, n, 7)
                elif slot == 1:
                    pe.wait_ge(k_final, HA + 1 + n)
                    turn(k, HG, n, K_FILL[HG])
                elif slot == 2:
                    hgrn_out(n)
                elif slot == 3:
                    hgrn_squares(n)
                elif slot == 4:
                    hgrn_prompt_states(n)
                elif slot < 7:
                    hgrn_states(n, slot - 5)

            def hgrn_pair(n, tail):
                m = M_HG + 2 * n
                for u in range(UNITS):
                    unit(m, 1, u, a_hi, a_lo)
                    if tail:
                        hgrn_tail(n - 1, u)
                for u in range(UNITS):
                    unit(m + 1, 0, u, a_hi, a_lo)
                    if tail:
                        hgrn_tail(n - 1, 4 + u)
                for u in range(UNITS):
                    unit(m + 1, 1, u, a_hi, a_lo)
                    if u > 0:
                        scores(HG, n, u - 1)
                for u in range(UNITS):
                    unit(m + 2, 0, u, a_hi, a_lo)
                    scores(HG, n, 3 + u)
                    if u == 2:
                        slab_read(pe, m + 1, 1)
                        turn(v_t, HG, n, V_FILL[HG])

            def merge_a(n, tail):
                for u in range(UNITS):
                    unit(M_MA + n, 1, u, a_hi, a_lo)
                    if tail:
                        gla_tail(HA - 1, u)
                for u in range(UNITS):
                    pe.wait_ge(heads_ready, u + 1)
                    unit(M_MA + n + 1, 0, u, b_hi, b_lo)
                    if tail and u == 0:
                        gla_tail(HA - 1, 4)

            def merge_b(n, tail):
                for u in range(UNITS):
                    unit(M_MB + n, 1, u, a_hi, a_lo)
                    if tail:
                        hgrn_tail(HPAIRS - 1, u)
                for u in range(UNITS):
                    pe.wait_ge(heads_ready, HA + 2 * (u + 1))
                    unit(M_MB + n + 1, 0, u, b_hi, b_lo)
                    if tail:
                        hgrn_tail(HPAIRS - 1, 4 + u)

            def sum_squares(value, fill):
                pe.wait_ge(sq_summed, value)
                pe.wait_ge(free[0], fill)
                for j in range(2):
                    ins = small(spare[0][:, 0:T], ones[:], sq_sum[:, j, :], j == 0, j == 1)
                ins.then_inc(full[0], 1)

            pe.wait_ge(consts_in, 16 * 5)
            for c in range(4):
                pe.wait_ge(sq_in_made, c + 1)
                for i in range(4):
                    ins = small(spare[0][:, 0:T], ones[:], sq_in[:, 4 * (c % 2) + i, :], c + i == 0, c + i == 6)
                ins.then_inc(sq_in_read if c < 3 else full[0], 1)
            for u in range(UNITS):
                pe.wait_ge(h_ready, u + 1)
                unit(0, 0, u, a_hi, a_lo, blocks=1)
            slab_read(pe, 0, 0)
            gla_head(0, False)
            with pe.Fori(1, HA) as h:
                gla_head(h, True)
            merge_a(0, True)
            with pe.Fori(1, NS2) as n:
                merge_a(n, False)
            hgrn_pair(0, False)
            with pe.Fori(1, HPAIRS) as n:
                hgrn_pair(n, True)
            merge_b(0, True)
            with pe.Fori(1, NS2) as n:
                merge_b(n, False)
            with pe.Fori(0, NS2 // 2) as n:
                for u in range(UNITS):
                    pe.wait_ge(merged_ready, u + 1)
                    unit(M_OUT + n, 1, u, a_hi, a_lo)
                for u in range(UNITS):
                    unit(M_OUT + n + 1, 0, u, a_hi, a_lo)
            sum_squares(NS2, LATE)
            with pe.Fori(0, QUARTERS) as c:
                with pe.Fori(0, NS2 // 2) as n:
                    for u in range(UNITS):
                        pe.wait_ge(res_ready, 2 * (u + 1))
                        unit(M_UP + M_Q * c + n, 1, u, b_hi, b_lo)
                    for u in range(UNITS):
                        unit(M_UP + M_Q * c + n + 1, 0, u, b_hi, b_lo)
                with pe.Fori(0, NS2 // 2) as n:
                    for u in range(UNITS):
                        pe.wait_ge(hid_ready, c * NS2 + 2 * (u + 1))
                        unit(M_DOWN + M_Q * c + n, 1, u, a_hi, a_lo)
                    for u in range(UNITS):
                        unit(M_DOWN + M_Q * c + n + 1, 0, u, a_hi, a_lo)
            sum_squares(2 * NS2, LATE + 1)

        @block.scalar
        def _(act):
            me = Tally(act, act_self)

            def split(m, par, u):
                slot = 2 * par + u // 2
                if not isinstance(m, int) or m + par > 0:
                    act.wait_ge(mm_done, 8 * m + (4 * par + u - 3))
                act.wait_ge(raw_in[slot], 16 * (m + 1))
                act.activation(w_hi[:, u, :, :], raw[:, slot, (u % 2) * UK:(u % 2 + 1) * UK, :], ACT.Copy)\
                   .then_inc(hi_made, 1)

            def filled(bank, phase, n, fill):
                act.wait_ge(full[bank], fills(bank, phase, n, fill) + 1)

            def slab_out(m, par, out, func, scale=1.0, release=True):
                slab_done(act, m, par)
                ins = act.activation(out, acc[par][:, :, 0:T], func, scale=scale)
                ins.then_inc(acc_free[par] if release else sig_made, 1)

            def from_turned(dst, at, phase, n, fill):
                for j in range(2):
                    filled(2 + j, phase, n, fill)
                    cols = slice(at + j * P, at + (j + 1) * P)
                    act.activation(dst[:, 0:2, cols], spare[2 + j][:, 0:NPR].rearrange("p (a b) -> p a b", b=P),
                                   ACT.Copy)
                    act.activation(dst[0:NSM, 2, cols], spare[2 + j][0:NSM, NPR:NPR + P], ACT.Copy)\
                       .then_inc(free[2 + j], 1)

            def root(view):
                act.activation(view, view, ACT.Sqrt).then_inc(root_made, 1)

            def head_hi(phase, n, tiles):
                act.wait_ge(on_made, per(phase, n, 1, 1, 1))
                act.activation(b_hi[:, tiles, :], o_sb[phase], ACT.Copy).then_inc(on_hi, 1)

            def gla_tail(h, slot):
                if slot == 2:
                    filled(1, GLA, h, 3)
                    ins = act.activation(o_sb[GLA][:, :, NPR:T],
                                         spare[1][:, 0:4 * NSM].rearrange("p (v t) -> p v t", v=4), ACT.Copy)
                    ins.then_inc(free[1], 1)
                    was_read(act, 1, GLA, h, 3)
                    filled(3, GLA, h, 11)
                    act.activation(sq[GLA], o_sb[GLA], ACT.Square).then_inc(sq_made, 1)
                if slot == 3:
                    was_read(act, 0, GLA, h, 9)
                    root(norm[:, 0, :])
                    head_hi(GLA, h, bass.ds(4 * h, 4))
                if slot == 4:
                    wait_from(act, ps_out, 16 * h)
                    for j in range(2):
                        filled(2 + j, GLA, h, 12)
                        act.activation(ps_gla[:, j, :], spare[2 + j][:, :], ACT.Copy).then_inc(free[2 + j], 1)

            def gla_gate(h):
                wait_from(act, level_ready, LEVELS * h)
                for j in range(2):
                    filled(j, GLA, h, 0)
                    act.activation(g[:, j, :], spare[j][:, 0:T], ACT.Identity,
                                   bias=vec[:, bass.ds(2 * h + (V_BG + j), 1)]).then_inc(free[j], 1)
                was_read(act, 1, GLA, h, 0)
                me.link(act.activation(q_raw, g, ACT.Abs))
                me.link(act.activation(q_raw, q_raw, ACT.Exp, scale=-1.0))
                act.activation(q_raw, q_raw, ACT.Ln, bias=1.0).then_inc(soft_made, 1)
                act.wait_ge(log_made, h + 1)
                act.activation(g, g, ACT.Exp, scale=1.0 / GATE_NORM).then_inc(g_made, 1)

            def gla_head(h, tail):
                m = M_GLA + 3 * h
                for u in range(UNITS):
                    split(m + 1, 0, u)
                    if tail:
                        gla_tail(h - 1, u)
                slab_out(m, 1, k, ACT.Copy)
                for u in range(UNITS):
                    split(m + 1, 1, u)
                    if tail and u == 0:
                        gla_tail(h - 1, 4)
                    if u == 1:
                        gla_gate(h)
                slab_out(m + 1, 0, q_raw, ACT.Copy, scale=DKA ** -0.5)
                for u in range(UNITS):
                    split(m + 2, 0, u)
                wait_from(act, heads_ready, h)
                slab_out(m + 1, 1, v_t, ACT.Copy)
                for u in range(UNITS):
                    split(m + 2, 1, u)
                    if u == 2:
                        from_turned(v_tok[GLA], 0, GLA, h, V_FILL[GLA])
                slab_out(m + 2, 0, v_t, ACT.Copy)
                for u in range(UNITS):
                    split(m + 3, 0, u)
                    if u == 1:
                        from_turned(v_tok[GLA], 256, GLA, h, V_FILL[GLA] + 1)
                    if u == 2:
                        from_turned(k_tok, 0, GLA, h, K_FILL[GLA])
                slab_out(m + 2, 1, r_sb[GLA][:, 0:2, :], ACT.Sigmoid, release=False)
                for u in range(UNITS):
                    split(m + 3, 1, u)
                    filled(0, GLA, h, 5 + u)
                    act.activation(o_sb[GLA][:, u, 0:NPR], spare[0][:, 0:NPR], ACT.Copy).then_inc(free[0], 1)
                slab_out(m + 3, 0, r_sb[GLA][:, 2:4, :], ACT.Sigmoid, release=False)

            def hgrn_tail(n, slot):
                if slot == 1:
                    from_turned(k_tok, 0, HG, n, K_FILL[HG])
                if slot == 2:
                    for j in range(2):
                        filled(j, HG, n, 4 - j)
                        act.activation(o_sb[HG][:, j, :], spare[j][:, 0:T], ACT.Copy)
                        act.activation(sq[HG][:, j, :], spare[j][:, 0:T], ACT.Square).then_inc(free[j], 1)
                if slot == 3:
                    was_read(act, 3, HG, n, 3)
                    root(norm)
                    head_hi(HG, n, bass.ds(2 * n, 2))
                if slot == 4:
                    act.wait_ge(ps_out, 16 * per(HG, n, 1, 1, 0))
                    filled(0, HG, n, 5)
                    act.activation(ps_hg, spare[0][:, 0:2 * P].rearrange("p (j v) -> p j v", j=2), ACT.Copy)\
                       .then_inc(free[0], 1)

            def hgrn_pair(n, tail):
                m = M_HG + 2 * n
                for u in range(UNITS):
                    split(m + 1, 0, u)
                    if tail:
                        hgrn_tail(n - 1, u)
                act.wait_ge(level_ready, per(HG, n, LEVELS, LEVELS, 0))
                slab_out(m, 1, g, ACT.Sigmoid)
                for u in range(UNITS):
                    split(m + 1, 1, u)
                    if tail:
                        hgrn_tail(n - 1, 4 + u)
                act.wait_ge(heads_ready, per(HG, n, 1, 1, 0))
                slab_out(m + 1, 0, v_t, ACT.Sigmoid, release=False)
                for u in range(UNITS):
                    split(m + 2, 0, u)
                slab_read(act, m + 1, 0)
                slab_out(m + 1, 1, v_t, ACT.Copy)
                for u in range(UNITS):
                    split(m + 2, 1, u)
                    if u == 2:
                        from_turned(v_tok[HG], 0, HG, n, V_FILL[HG])
                slab_out(m + 2, 0, r_sb[HG], ACT.Sigmoid, release=False)

            def merge_a(n, tail):
                for u in range(UNITS):
                    split(M_MA + n + 1, 0, u)
                    if tail:
                        gla_tail(HA - 1, u)
                slab_read(act, M_MA + n, 0)
                slab_out(M_MA + n, 1, gate, ACT.Sigmoid)
                for u in range(UNITS):
                    split(M_MA + n + 1, 1, u)
                    if tail and u == 0:
                        gla_tail(HA - 1, 4)

            def merge_b(n, tail):
                for u in range(UNITS):
                    split(M_MB + n + 1, 0, u)
                    if tail:
                        hgrn_tail(HPAIRS - 1, u)
                wait_from(act, merged, n)
                slab_out(M_MB + n, 1, gate, ACT.Sigmoid)
                for u in range(UNITS):
                    split(M_MB + n + 1, 1, u)
                    if tail:
                        hgrn_tail(HPAIRS - 1, 4 + u)

            def squares(m, par, tile, index):
                wait_apart(act, acc_free[par], m + 1)
                wait_apart(act, sq_summed, index)
                act.activation(sq_new, m_sb[:, bass.ds(tile, 2), :], ACT.Square).then_inc(res_sq, 1)

            def out_end(m, par, index):
                slab_read(act, m, par)
                for j in range(2):
                    ins = act.activation(b_hi[:, bass.ds(2 * index + j, 1), :], m_sb[:, bass.ds(2 * index + j, 1), :],
                                         ACT.Copy, scale=vec[:, bass.ds(2 * index + (V_MLP + j), 1)])
                ins.then_inc(res_hi, 1)
                squares(m, par, 2 * index, index)

            def up_end(m, par, index, c):
                act.wait_ge(hid_ready, c * NS2 + index)
                slab_read(act, m, par)
                me.link(act.activation(hid_f, hid_t, ACT.Square))
                act.activation(a_hi[:, bass.ds(2 * index, 2), :], hid_f, ACT.Copy).then_inc(hid_hi, 1)

            def up(c):
                with me.loop(0, NS2 // 2, 2) as n:
                    m = M_UP + M_Q * c + n
                    for u in range(UNITS):
                        split(m + 1, 0, u)
                    up_end(m, 1, 2 * n, c)
                    for u in range(UNITS):
                        split(m + 1, 1, u)
                    up_end(m + 1, 0, 2 * n + 1, c)

            def down(n, c, last, end):
                m = M_DOWN + M_Q * c + n
                for u in range(UNITS):
                    split(m + 1, 0, u)
                if last:
                    squares(m, 1, 4 * n, 2 * n + NS2)
                for u in range(UNITS):
                    if not end:
                        split(m + 1, 1, u)
                if last:
                    squares(m + 1, 0, 4 * n + 2, 2 * n + (NS2 + 1))

            for c in range(4):
                act.wait_ge(x_in[c], 16)
                if c >= 2:
                    act.wait_ge(sq_in_read, c - 1)
                act.activation(sq_in[:, 4 * (c % 2):4 * (c % 2) + 4, :], m_sb[:, 4 * c:4 * c + 4, :], ACT.Square)\
                   .then_inc(sq_in_made, 1)
            for u in range(UNITS):
                split(0, 0, u)
            act.wait_ge(free[0], 1)
            root(norm[:, 0, :])
            for c in range(4):
                act.wait_ge(h_made, c + 1)
                act.activation(a_hi[:, 4 * c:4 * c + 4, :], m_sb[:, 4 * c:4 * c + 4, :], ACT.Copy).then_inc(h_hi, 1)
            act.wait_ge(lb_max, 1)
            act.activation(soft[:, 0:2, :], soft[:, 0:2, :], ACT.Exp).then_inc(lb_exp, 1)
            for u in range(UNITS):
                split(0, 1, u)
            slab_done(act, 0, 0)
            act.activation(gr[:], acc[0][0:RANK, 0, 0:T], ACT.Copy).then_inc(acc_free[0], 1)
            gla_head(0, False)
            with me.loop(1, HA, 2) as h:
                gla_head(h, True)
            merge_a(0, True)
            with act.Fori(1, NS2) as n:
                merge_a(n, False)
            hgrn_pair(0, False)
            with act.Fori(1, HPAIRS) as n:
                hgrn_pair(n, True)
            merge_b(0, True)
            with act.Fori(1, NS2) as n:
                merge_b(n, False)
            for c in range(4):
                act.wait_ge(merged, NS2)
                act.activation(a_hi[:, 4 * c:4 * c + 4, :], m_sb[:, 4 * c:4 * c + 4, :], ACT.Copy)\
                   .then_inc(merged_hi, 1)
            with act.Fori(0, NS2 // 2) as n:
                for u in range(UNITS):
                    split(M_OUT + n + 1, 0, u)
                out_end(M_OUT + n, 1, 2 * n)
                for u in range(UNITS):
                    split(M_OUT + n + 1, 1, u)
                out_end(M_OUT + n + 1, 0, 2 * n + 1)
            act.wait_ge(free[0], LATE + 1)
            root(norm[:, 0, :])
            with me.loop(0, QUARTERS - 1, NS2) as c:
                up(c)
                with act.Fori(0, NS2 // 2) as n:
                    down(n, c, False, False)
            up(QUARTERS - 1)
            with act.Fori(0, NS2 // 2 - 1) as n:
                down(n, QUARTERS - 1, True, False)
            down(NS2 // 2 - 1, QUARTERS - 1, True, True)
            act.wait_ge(free[0], LATE + 2)
            root(norm[:, 0, :])

        @block.vector
        def _(dve):
            me = Tally(dve, dve_self)

            def split(m, par, u):
                slot = 2 * par + u // 2
                if not isinstance(m, int) or m + par > 0:
                    dve.wait_ge(mm_done, 8 * m + (4 * par + u - 3))
                dve.wait_ge(hi_made, 8 * m + (4 * par + u + 1))
                dve.tensor_tensor(w_lo[:, u, :, :], raw[:, slot, (u % 2) * UK:(u % 2 + 1) * UK, :],
                                  w_hi[:, u, :, :].bitcast(F32), ALU.subtract).then_inc(lo_made, 1)

            def filled(bank, phase, n, fill):
                dve.wait_ge(full[bank], fills(bank, phase, n, fill) + 1)

            def mean(out, bank, count):
                return dve.tensor_scalar(out, spare[bank][:, 0:T], 1.0 / count, EPS, ALU.mult, ALU.add)

            def block_decays():
                for level in range(1, LEVELS):
                    n = TOT_N[level]
                    pairs = tot(level - 1)[:, :, 0:2 * n].rearrange("p j (n h) -> p j n h", h=2)
                    me.link(dve.tensor_tensor(tot(level), pairs[:, :, :, 0], pairs[:, :, :, 1], ALU.mult))

            def level(phase, n, lv):
                heads = 2 if phase == HG else 1
                bank, fill = level_bank(phase, lv)
                for h in range(heads):
                    src = spare[h] if lv == 0 else spare[bank]
                    if lv == 0 or h == 0:
                        at = h if lv == 0 else bank
                        wait_apart(dve, full[at], fills(at, phase, n, fill) + 1)
                    at = T if lv == 0 else 160 * h
                    if lv == 0:
                        for rows, col, to in ((P, 0, 0), (P, P, NPR), (NSM, NPR, NPR + P)):
                            ins = dve.copy_predicated(sc[0:rows, h, to:to + rows], masks[0:rows, 0:rows],
                                                      src[0:rows, col:col + rows])
                        me.link(ins, wait_apart)
                    if lv < 6:
                        mask = masks[:, P + 64 * lv:P + 64 * (lv + 1)]
                        for tt, (rows, size) in enumerate(((P, 64), (P, 64), (NSM, 32))[:3 if lv < 3 else 2]):
                            to = (0, NPR, NPR + P)[tt]
                            out = halves(sc[0:rows, h, to:to + 2 * size], lv)[:, :, 1, :]
                            ins = dve.copy_predicated(
                                out, mask[0:rows, 0:size].rearrange("p (n b) -> p n b", b=1 << lv),
                                src[0:rows, at + 64 * tt:at + 64 * tt + size]
                                .rearrange("p (n b) -> p n b", b=1 << lv))
                    elif lv == 6:
                        for tt in range(2):
                            ins = dve.tensor_copy(sc[0:64, h, NPR * tt + 64:NPR * tt + P],
                                                  src[0:64, at + 64 * tt:at + 64 * (tt + 1)])
                    else:
                        ins = dve.tensor_copy(sc[:, h, P:NPR], src[:, at:at + P])
                    if lv == 0 and heads == 2:
                        ins.then_inc(free[h], 1)
                if not (lv == 0 and heads == 2):
                    ins.then_inc(free[bank], 1)
                end = T if lv < 3 else NPR
                pairs = tot(lv)[:, :, 0:end >> lv].rearrange("p j (n h) -> p j n h", h=2)
                shape = [P, 2, end >> (lv + 1), 1 << lv]
                second = halves(q[:, :, 0:end], lv)[:, :, :, 1, :]
                first = halves(k[:, :, 0:end], lv)[:, :, :, 0, :]
                if lv < LEVELS - 1:
                    dve.tensor_tensor(second, second, pairs[:, :, :, 0:1].to_broadcast(shape), ALU.mult)
                dve.tensor_tensor(first, first, pairs[:, :, :, 1:2].to_broadcast(shape), ALU.mult)\
                   .then_inc(level_ready if lv < LEVELS - 1 else k_final, 1)

            def head_end(phase, n, tiles, r_slab):
                dve.wait_ge(root_made, per(phase, n, 1, 1, 2))
                used = norm[:, 0, :] if phase == GLA else norm
                me.link(dve.reciprocal(used, used))
                o = o_sb[phase]
                if phase == GLA:
                    for v in range(4):
                        ins = dve.scalar_tensor_tensor(out=o[:, v, :], in0=o[:, v, :], in1=used,
                                                       scalar=vec[:, V_GA + v:V_GA + v + 1], op0=ALU.mult,
                                                       op1=ALU.mult)
                else:
                    ins = dve.scalar_tensor_tensor(out=o, in0=o, scalar=vec[:, V_GB:V_GB + 1], in1=used,
                                                   op0=ALU.mult, op1=ALU.mult)
                me.link(ins)
                slab_read(dve, *r_slab)
                dve.tensor_tensor(o, o, r_sb[phase], ALU.mult).then_inc(on_made, 1)
                dve.wait_ge(on_hi, per(phase, n, 1, 1, 1))
                dve.tensor_tensor(b_lo[:, tiles, :], o, b_hi[:, tiles, :].bitcast(F32), ALU.subtract)\
                   .then_inc(heads_ready, 1)

            def swish(m, par, out, sig, sig_count):
                dve.wait_ge(sig_made, sig_count)
                dve.tensor_tensor(out, acc[par][:, :, 0:T], sig, ALU.mult).then_inc(acc_free[par], 1)

            def gla_state(h, b):
                for j in range(2):
                    filled(2 + j, GLA, h, 4 + b)
                    st = st_gla[b % 4][:, j, :]
                    dve.scalar_tensor_tensor(out=st, in0=st, scalar=own_tot(j, b), in1=spare[2 + j][:, :],
                                             op0=ALU.mult, op1=ALU.add).then_inc(free[2 + j], 1)

            def gla_tail(h, slot):
                if slot < 3:
                    gla_state(h, 5 + slot)
                if slot == 3:
                    filled(0, GLA, h, 9)
                    mean(norm[:, 0, :], 0, DVA).then_inc(free[0], 1)
                    head_end(GLA, h, bass.ds(4 * h, 4), (M_GLA + 3 * h + 3, 0))

            def gla_head(h, tail):
                m = M_GLA + 3 * h
                for u in range(UNITS):
                    split(m + 1, 0, u)
                    if tail:
                        gla_tail(h - 1, u)
                for u in range(UNITS):
                    split(m + 1, 1, u)
                    if u == 1:
                        dve.wait_ge(soft_made, h + 1)
                        dve.scalar_tensor_tensor(out=g, in0=g, scalar=0.0, in1=q_raw, op0=ALU.min,
                                                 op1=ALU.subtract).then_inc(log_made, 1)
                    if u == 2:
                        dve.wait_ge(g_made, h + 1)
                        block_decays()
                slab_read(dve, m + 1, 0)
                dve.tensor_tensor(q, q_raw, g, ALU.mult).then_inc(level_ready, 1)
                for u in range(UNITS):
                    split(m + 2, 0, u)
                    if u > 0:
                        level(GLA, h, u - 1)
                for u in range(UNITS):
                    split(m + 2, 1, u)
                    level(GLA, h, 3 + u)
                for u in range(UNITS):
                    split(m + 3, 0, u)
                    if u == 0:
                        level(GLA, h, 7)
                    if u == 3:
                        gla_state(h, 0)
                swish(m + 2, 1, r_sb[GLA][:, 0:2, :], r_sb[GLA][:, 0:2, :], 2 * h + 1)
                for u in range(UNITS):
                    split(m + 3, 1, u)
                    gla_state(h, 1 + u)
                swish(m + 3, 0, r_sb[GLA][:, 2:4, :], r_sb[GLA][:, 2:4, :], 2 * h + 2)

            def hgrn_tail(n, slot):
                if slot == 0:
                    level(HG, n, 7)
                if slot == 3:
                    for j in range(2):
                        filled(2 + j, HG, n, 3)
                        mean(norm[:, j, :], 2 + j, P).then_inc(free[2 + j], 1)
                    head_end(HG, n, bass.ds(2 * n, 2), (M_HG + 2 * n + 2, 0))
                if slot in (5, 6):
                    j = slot - 5
                    for half in range(2):
                        bank, fill = ((2 + half, 4), (half, (6, 4)[half]))[j]
                        filled(bank, HG, n, fill)
                        for b in range(4):
                            st = st_hg[:, j, 4 * half + b, :]
                            ins = dve.scalar_tensor_tensor(out=st, in0=st, scalar=own_tot(j, 4 * half + b),
                                                           in1=spare[bank][:, b * P:(b + 1) * P],
                                                           op0=ALU.mult, op1=ALU.add)
                        ins.then_inc(free[bank], 1)

            def hgrn_pair(n, tail):
                m = M_HG + 2 * n
                for u in range(UNITS):
                    split(m + 1, 0, u)
                    if tail:
                        hgrn_tail(n - 1, u)
                dve.wait_ge(full[3], fills(3, HG, n - 1, K_FILL[HG]) + 1 if tail
                            else fills(3, GLA, HA - 1, K_FILL[GLA]) + 1)
                slab_read(dve, m, 1)
                for j in range(2):
                    ins = dve.tensor_scalar(g[:, j, :], g[:, j, :], one_lb[:, bass.ds(2 * n + j, 1)],
                                            lb[:, bass.ds(2 * n + j, 1)], ALU.mult, ALU.add)
                me.link(ins)
                dve.tensor_scalar(k, g, -1.0, 1.0, ALU.mult, ALU.add)
                for u in range(UNITS):
                    split(m + 1, 1, u)
                    if tail:
                        hgrn_tail(n - 1, 4 + u)
                block_decays()
                swish(m + 1, 0, q_raw, v_t, per(HG, n, 2, 2, 1))
                slab_read(dve, m + 1, 0)
                dve.tensor_tensor(q, q_raw, g, ALU.mult).then_inc(level_ready, 1)
                for u in range(UNITS):
                    split(m + 2, 0, u)
                    if u > 0:
                        level(HG, n, u - 1)
                for u in range(UNITS):
                    split(m + 2, 1, u)
                    level(HG, n, 3 + u)
                swish(m + 2, 0, r_sb[HG], r_sb[HG], per(HG, n, 2, 2, 2))

            def merge_a(n, tail):
                for u in range(UNITS):
                    split(M_MA + n + 1, 0, u)
                    if tail:
                        gla_tail(HA - 1, u)
                for u in range(UNITS):
                    split(M_MA + n + 1, 1, u)
                if tail:
                    for b in range(4):
                        dve.wait_ge(st_out[b], 16 * 2 * HA)
                    dve.wait_ge(ps_out, 16 * HA)
                slab_read(dve, M_MA + n, 1)
                slab_done(dve, M_MA + n + 1, 0)
                dve.tensor_tensor(m_sb[:, bass.ds(2 * n, 2), :], acc[0][:, :, 0:T], gate, ALU.mult)\
                   .then_inc(acc_free[0], 1)

            def merge_b(n, tail):
                for u in range(UNITS):
                    split(M_MB + n + 1, 0, u)
                    if tail:
                        hgrn_tail(HPAIRS - 1, u)
                for u in range(UNITS):
                    split(M_MB + n + 1, 1, u)
                    if tail:
                        hgrn_tail(HPAIRS - 1, 4 + u)
                slab_read(dve, M_MB + n, 1)
                slab_done(dve, M_MB + n + 1, 0)
                dve.tensor_tensor(gate, acc[0][:, :, 0:T], gate, ALU.mult).then_inc(acc_free[0], 1)
                slab_read(dve, M_MB + n + 1, 0)
                tile = m_sb[:, bass.ds(2 * n, 2), :]
                dve.tensor_tensor(tile, tile, gate, ALU.add).then_inc(merged, 1)

            def add_squares(index):
                dve.wait_ge(res_sq, index + 1)
                dve.wait_ge(sq_summed, index)
                dve.tensor_tensor(sq_sum, sq_sum, sq_new, ALU.add).then_inc(sq_summed, 1)

            def out_end(m, par, index):
                slab_done(dve, m, par)
                dve.tensor_tensor(m_sb[:, bass.ds(2 * index, 2), :], acc[par][:, :, 0:T],
                                  x_res[:, bass.ds(2 * index, 2), :], ALU.add).then_inc(acc_free[par], 1)
                dve.wait_ge(res_hi, index + 1)
                for j in range(2):
                    at = bass.ds(2 * index + j, 1)
                    ins = dve.scalar_tensor_tensor(out=b_lo[:, at, :], in0=m_sb[:, at, :],
                                                   scalar=vec[:, bass.ds(2 * index + (V_MLP + j), 1)],
                                                   in1=b_hi[:, at, :].bitcast(F32), op0=ALU.mult,
                                                   op1=ALU.subtract)
                ins.then_inc(res_ready, 1)
                add_squares(index)

            def up_end(m, par, index, c):
                slab_done(dve, m, par)
                dve.scalar_tensor_tensor(out=hid_t, in0=acc[par][:, :, 0:T], scalar=0.0,
                                         in1=norm[:, 0:1, :].to_broadcast([P, 2, T]), op0=ALU.max,
                                         op1=ALU.mult).then_inc(acc_free[par], 1)
                dve.wait_ge(hid_hi, c * NS2 + index + 1)
                at = bass.ds(2 * index, 2)
                dve.tensor_tensor(a_lo[:, at, :], hid_f, a_hi[:, at, :].bitcast(F32), ALU.subtract)\
                   .then_inc(hid_ready, 1)

            def up(c):
                with dve.Fori(0, NS2 // 2) as n:
                    m = M_UP + M_Q * c + n
                    for u in range(UNITS):
                        split(m + 1, 0, u)
                    up_end(m, 1, 2 * n, c)
                    for u in range(UNITS):
                        split(m + 1, 1, u)
                    up_end(m + 1, 0, 2 * n + 1, c)

            def down_end(m, par, tile):
                slab_done(dve, m, par)
                dve.wait_ge(acc_free[par], m)
                at = m_sb[:, bass.ds(tile, 2), :]
                dve.tensor_tensor(at, at, acc[par][:, :, 0:T], ALU.add).then_inc(acc_free[par], 1)

            def down(n, c, last, end):
                m = M_DOWN + M_Q * c + n
                for u in range(UNITS):
                    split(m + 1, 0, u)
                down_end(m, 1, 4 * n)
                if last:
                    add_squares(2 * n + NS2)
                for u in range(UNITS):
                    if not end:
                        split(m + 1, 1, u)
                down_end(m + 1, 0, 4 * n + 2)
                if last:
                    add_squares(2 * n + (NS2 + 1))

            def stream_norm(count, roots):
                dve.wait_ge(full[0], count)
                mean(norm[:, 0, :], 0, D).then_inc(free[0], 1)
                dve.wait_ge(root_made, roots)
                me.link(dve.reciprocal(norm[:, 0, :], norm[:, 0, :]))

            for u in range(UNITS):
                split(0, 0, u)
            dve.memset(sc, 0.0)
            dve.wait_ge(consts_in, 16 * 5)
            dve.tensor_copy(masks[:], masks_f)
            first, second, most = vec[:, V_LB0:V_LB0 + KT], vec[:, V_LB1:V_LB1 + KT], soft[:, 2, :]
            me.link(dve.tensor_tensor(most, first, second, ALU.max))
            dve.tensor_tensor(soft[:, 0, :], first, most, ALU.subtract)
            dve.tensor_tensor(soft[:, 1, :], second, most, ALU.subtract).then_inc(lb_max, 1)
            stream_norm(1, 1)
            for c in range(5):
                if c < 4:
                    for i in range(4):
                        tile = m_sb[:, 4 * c + i, :]
                        ins = dve.scalar_tensor_tensor(out=tile, in0=tile, scalar=vec[:, V_MIX + 4 * c + i:][:, 0:1],
                                                       in1=norm[:, 0, :], op0=ALU.mult, op1=ALU.mult)
                    ins.then_inc(h_made, 1)
                if c > 0:
                    at = slice(4 * c - 4, 4 * c)
                    dve.wait_ge(h_hi, c)
                    dve.tensor_tensor(a_lo[:, at, :], m_sb[:, at, :], a_hi[:, at, :].bitcast(F32), ALU.subtract)\
                       .then_inc(h_ready, 1)
            dve.wait_ge(lb_exp, 1)
            me.link(dve.tensor_tensor(most, soft[:, 0, :], soft[:, 1, :], ALU.add))
            me.link(dve.reciprocal(most, most))
            me.link(dve.tensor_tensor(lb[:], soft[:, 0, :], most, ALU.mult))
            me.link(dve.tensor_scalar(one_lb[:], lb[:], -1.0, 1.0, ALU.mult, ALU.add))
            for u in range(UNITS):
                split(0, 1, u)
            gla_head(0, False)
            with me.loop(1, HA, LEVELS - 1 + 3) as h:
                gla_head(h, True)
            merge_a(0, True)
            with dve.Fori(1, NS2) as n:
                merge_a(n, False)
            hgrn_pair(0, False)
            with me.loop(1, HPAIRS, LEVELS - 1 + 5) as n:
                hgrn_pair(n, True)
            merge_b(0, True)
            with dve.Fori(1, NS2) as n:
                merge_b(n, False)
            for c in range(4):
                at = slice(4 * c, 4 * c + 4)
                dve.wait_ge(merged_hi, c + 1)
                dve.tensor_tensor(a_lo[:, at, :], m_sb[:, at, :], a_hi[:, at, :].bitcast(F32), ALU.subtract)\
                   .then_inc(merged_ready, 1)
            me.link(dve.memset(sq_sum, 0.0))
            dve.wait_ge(x_res_in, 16)
            with dve.Fori(0, NS2 // 2) as n:
                for u in range(UNITS):
                    split(M_OUT + n + 1, 0, u)
                out_end(M_OUT + n, 1, 2 * n)
                for u in range(UNITS):
                    split(M_OUT + n + 1, 1, u)
                out_end(M_OUT + n + 1, 0, 2 * n + 1)
            stream_norm(LATE + 1, HA + HPAIRS + 2)
            me.link(dve.memset(sq_sum, 0.0))
            with dve.Fori(0, QUARTERS - 1) as c:
                up(c)
                with dve.Fori(0, NS2 // 2) as n:
                    down(n, c, False, False)
            up(QUARTERS - 1)
            with dve.Fori(0, NS2 // 2 - 1) as n:
                down(n, QUARTERS - 1, True, False)
            down(NS2 // 2 - 1, QUARTERS - 1, True, True)
            stream_norm(LATE + 2, HA + HPAIRS + 3)
            for i in range(KT):
                tile = m_sb[:, i, :]
                ins = dve.scalar_tensor_tensor(out=tile, in0=tile, scalar=vec[:, V_FIN + i:V_FIN + i + 1],
                                               in1=norm[:, 0, :], op0=ALU.mult, op1=ALU.mult)
                if i % 2:
                    ins.then_inc(y_made, 1)


def _masks():
    import numpy as np

    s = np.arange(P)[:, None]
    out = [s == np.arange(P)[None, :]]
    for level in range(6):
        t = np.array([x for x in range(P) if x >> level & 1])[None, :]
        out.append((s >> (level + 1) == t >> (level + 1)) & (s >> level & 1 == 0))
    return np.concatenate(out, axis=1).astype(np.float32)


def kernel(**inputs):
    import numpy as np

    import concourse.bacc as bacc
    from concourse.bass_utils import run_bass_kernel_spmd

    a = {name: np.asarray(value) for name, value in inputs.items()}
    tokens = np.concatenate([a["x_prompt"].reshape(NPR, D), a["x_sample"].reshape(NSM, D)])
    rows = [a["norm_mix"], a["norm_mlp"], a["norm_final"], a["hg_lower_bound"], a["b_gate2"], a["gla_norm"],
            a["hg_norm"]]
    arrays = {
        "x_t": tokens.T,
        "state_gla": a["state_gla"][0],
        "state_hgrn": a["state_hgrn"][0],
        "vectors": np.concatenate([r.reshape(-1, P) for r in rows]).T,
        "w_in": a["w_in"][0],
        "w_gate2": a["w_gate2"][0],
        "w_branch_a": a["w_branch_a"][0],
        "w_branch_b": a["w_branch_b"][0],
        "w_out": a["w_out"][0],
        "w_up": a["w_up"][0],
        "w_down": a["w_down"][0],
        "ones_in": np.ones((P, P), np.float32),
        "eye_in": np.eye(P, dtype=np.float32),
        "own_in": np.repeat(np.eye(SB, dtype=np.float32), SL, axis=0),
        "masks_in": _masks(),
    }
    arrays = {f"{name}_dram": np.ascontiguousarray(value) for name, value in arrays.items()}
    outs = {"y_t": (D, T), "new_gla_prompt": (HA, DKA, DVA), "new_hgrn_prompt": (HB, P, P),
            "new_gla_sample": (SB, HA, DKA, DVA), "new_hgrn_sample": (SB, HB, P, P)}
    nc = bacc.Bacc("TRN2", target_bir_lowering=False, num_devices=1)
    args = [nc.dram_tensor(name, v.shape, mybir.dt.from_np(v.dtype), kind="ExternalInput").ap()
            for name, v in arrays.items()]
    args += [nc.dram_tensor(name, shape, F32, kind="ExternalOutput").ap() for name, shape in outs.items()]
    gated_merge_step(nc, *args)
    got = run_bass_kernel_spmd(nc, [arrays], core_ids=[0]).results[0]
    y = np.ascontiguousarray(got["y_t"].T)
    return (y[:NPR].reshape(1, NPR, D), y[NPR:].reshape(SB, SL, D),
            got["new_gla_prompt"].reshape(1, 1, HA, DKA, DVA), got["new_hgrn_prompt"].reshape(1, 1, HB, P, P),
            got["new_gla_sample"].reshape(1, SB, HA, DKA, DVA), got["new_hgrn_sample"].reshape(1, SB, HB, P, P))
```

```python
from contextlib import ExitStack, contextmanager

import concourse.bass as bass
from concourse import mybir

ALU = mybir.AluOpType
ACT = mybir.ActivationFunctionType
F32 = mybir.dt.float32
F32R = mybir.dt.float32r
U8 = mybir.dt.uint8

P = 128
D = 2048
KT = D // P
NPR = 256
SB, SL = 8, 8
NSM = SB * SL
T = NPR + NSM
HA, DKA, DVA = 4, 256, 512
HB = 16
HPAIRS = HB // 2
RANK = 16
FF = 4 * D
EPS = 1e-6
GATE_NORM = 16.0
W2 = 256
NS2 = D // W2
UNITS = 4
UK = KT // UNITS
QUARTERS = FF // D
SCRATCH = 9836
LEVELS = 8

C_QA, C_KA, C_VA, C_GR = 0, 1024, 2048, 4096
C_RA = C_GR + RANK
C_QB, C_FB, C_IB, C_RB, C_MA, C_MB = (C_RA + D * (1 + n) for n in range(6))

M_GLA, M_MA = 0, 3 * HA
M_HG = M_MA + NS2
M_MB = M_HG + 2 * HPAIRS
M_OUT = M_MB + NS2
M_UP = M_OUT + NS2 // 2
M_DOWN = M_UP + NS2 // 2
M_Q = NS2

V_MIX, V_MLP, V_FIN, V_LB0, V_LB1, V_BG, V_GA, V_GB = 0, 16, 32, 48, 64, 80, 88, 92
V_N = 93

GLA, HG = 0, 1
FILLS0 = (1, 0, 0, 0)
FILLS = ((10, 4, 13, 13), (7, 5, 5, 5))


def per(phase, n, gla, hg, k):
    return n * gla + k if phase == GLA else n * hg + (HA * gla + k)


def fills(bank, phase, n, k):
    return per(phase, n, FILLS[0][bank], FILLS[1][bank], k + FILLS0[bank])


def wait_from(eng, sem, value):
    if not isinstance(value, int) or value > 0:
        eng.wait_ge(sem, value)


class Tally:

    def __init__(self, eng, sem):
        self.eng, self.sem, self.before, self.here = eng, sem, 0, 0

    def link(self, ins, wait=None):
        ins.then_inc(self.sem, 1)
        self.here += 1
        if wait is None:
            self.eng.wait_ge(self.sem, self.before + self.here)
        else:
            wait(self.eng, self.sem, self.before + self.here)

    @contextmanager
    def loop(self, first, last, each):
        before, here = self.before, self.here
        with self.eng.Fori(first, last) as i:
            self.before, self.here = (i - first) * each + (before + here), 0
            yield i
        assert self.here == each, f"{self.here} links in a turn, not {each}"
        self.before, self.here = before, here + (last - first) * each


def gated_merge_step(nc, x_t, state_gla, state_hgrn, vectors, w_in, w_gate2, w_branch_a, w_branch_b, w_out,
                     w_up, w_down, ones_in, eye_in, own_in, masks_in,
                     y_t, gla_prompt, hgrn_prompt, gla_sample, hgrn_sample):
    ctx = ExitStack()
    with ctx:
        def sb(name, shape, dt=F32):
            return ctx.enter_context(nc.sbuf_tensor(name, shape, dt))

        def sem(name):
            return ctx.enter_context(nc.semaphore(name))

        raw = sb("raw", [P, 4, 2 * UK, W2])
        w_hi = sb("w_hi", [P, UNITS, UK, W2], F32R)
        w_lo = sb("w_lo", [P, UNITS, UK, W2], F32R)
        a_hi = sb("a_hi", [P, KT, T], F32R)
        a_lo = sb("a_lo", [P, KT, T], F32R)
        b_hi = sb("b_hi", [P, KT, T], F32R)
        b_lo = sb("b_lo", [P, KT, T], F32R)
        m_sb = sb("m_sb", [P, KT, T])
        s_sb = sb("s_sb", [P, SCRATCH])
        ones = sb("ones", [P, P])
        eye = sb("eye", [P, P])
        own = sb("own", [2 * NSM, SB])
        masks = sb("masks", [P, P + 6 * 64], U8)
        vec = sb("vec", [P, V_N])
        lb = sb("lb", [P, KT])
        one_lb = sb("one_lb", [P, KT])
        soft = sb("soft", [P, 3, KT])
        own_decays = sb("own_decays", [P, 2, SB])
        gr = sb("gr", [RANK, T])
        wg = sb("wg", [RANK, DKA])

        AT_Q = 2 * T
        AT_K = AT_Q + 2 * T
        AT_G = AT_K + 2 * T
        AT_TOT = AT_G + 2 * T
        AT_V = AT_TOT + 2 * 310
        AT_SC = AT_V + 2 * T
        AT_U = AT_SC + 2 * 448
        AT_PS = AT_U + 4096
        AT_KTOK = AT_PS + 2 * P
        assert AT_KTOK + 3 * DKA == SCRATCH == AT_U + KT * T

        def part(at, *shape):
            size = 1
            for x in shape:
                size *= x
            v = s_sb[:, at:at + size]
            if len(shape) == 2:
                v = v.rearrange("p (a b) -> p a b", b=shape[1])
            if len(shape) == 3:
                v = v.rearrange("p (a b c) -> p a b c", b=shape[1], c=shape[2])
            return v

        q_raw = part(0, 2, T)
        q = part(AT_Q, 2, T)
        k = part(AT_K, 2, T)
        g = part(AT_G, 2, T)
        tots = part(AT_TOT, 2, 310)
        v_t = part(AT_V, 2, T)
        sc = part(AT_SC, 2, 448)
        v_tok = [part(AT_U, 3, DVA), part(AT_U, 3, 256)]
        o_sb = [part(AT_U + 1536, 4, T), part(AT_U + 768, 2, T)]
        r_sb = [part(AT_U + 2816, 4, T), part(AT_U + 1408, 2, T)]
        st_hg = part(AT_U + 2048, 2, SB, P)
        ps_hg = part(AT_PS, 2, P)
        k_tok = part(AT_KTOK, 3, 256)
        x_res = part(AT_U, KT, T)
        k_own = part(0, 2, 512)
        b_hi_end = b_hi[:, KT - 4:KT, :].rearrange("p a b -> p (a b)")
        b_lo_end = b_lo[:, KT - 4:KT, :].rearrange("p a b -> p (a b)")
        v_parts = b_hi_end[:, 0:DVA]
        k_parts = b_hi_end[:, DVA:DVA + 2 * DKA]
        k_own_parts = [b_lo_end[:, n * 2 * DKA:(n + 1) * 2 * DKA] for n in range(2)]
        sq = [part(0, 4, T), part(0, 2, T)]
        norm = v_t
        guess = v_t[:, 1, :]

        def pair_guess(n):
            return b_lo[:, bass.ds(2 * n, 2), :]

        gate = k
        sq_sum, sq_new = part(0, 2, T), part(AT_Q, 2, T)
        hid_t, hid_f = k, g
        sq_in = [part(at, 4, T) for at in (0, 4 * T, AT_U + 512)]
        masks_f = part(AT_U, P + 6 * 64)
        m_flat = m_sb[:, :, :].rearrange("p a b -> p (a b)")
        st_gla = [m_flat[:, n * 1024:(n + 1) * 1024].rearrange("p (j v) -> p j v", j=2) for n in range(4)]
        ps_gla = m_flat[:, 4096:5120].rearrange("p (j v) -> p j v", j=2)

        TOT_AT = (None, 0, 160, 240, 280, 296, 304, 308)
        TOT_N = (T, 160, 80, 40, 16, 8, 4, 2)

        def tot(level):
            return g if level == 0 else tots[:, :, TOT_AT[level]:TOT_AT[level] + TOT_N[level]]

        def halves(v, level):
            if len(v.shape) == 3:
                return v.rearrange("p j (n h b) -> p j n h b", h=2, b=1 << level)
            return v.rearrange("p (n h b) -> p n h b", h=2, b=1 << level)

        def own_tot(j, b):
            at = TOT_AT[3] + NPR // SL + b
            return tots[:, j, at:at + 1]

        acc = [ctx.enter_context(nc.psum_tensor(f"acc{n}", [P, 2, 512], F32)) for n in range(2)]
        spare = [ctx.enter_context(nc.psum_tensor(f"spare{n}", [P, 512], F32)) for n in range(4)]

        ones_there = sem("ones_there")
        vec_there = sem("vec_there")
        consts_in = sem("consts_in")
        x_in = [sem(f"x_in{n}") for n in range(4)]
        x_res_in = sem("x_res_in")
        wg_in = sem("wg_in")
        raw_in = [sem(f"raw_in{n}") for n in range(4)]
        hi_made = sem("hi_made")
        lo_made = sem("lo_made")
        mm_done = sem("mm_done")
        acc_free = [sem(f"acc_free{n}") for n in range(2)]
        full = [sem(f"full{n}") for n in range(4)]
        free = [sem(f"free{n}") for n in range(4)]
        act_self = sem("act_self")
        dve_self = sem("dve_self")
        sq_in_made = sem("sq_in_made")
        sq_in_added = sem("sq_in_added")
        guess_made = sem("guess_made")
        norm_used = sem("norm_used")
        h_made = sem("h_made")
        h_hi = sem("h_hi")
        h_ready = sem("h_ready")
        lb_max = sem("lb_max")
        lb_exp = sem("lb_exp")
        soft_made = sem("soft_made")
        log_made = sem("log_made")
        g_made = sem("g_made")
        sig_made = sem("sig_made")
        level_ready = sem("level_ready")
        k_final = sem("k_final")
        k_own_made = sem("k_own_made")
        turned_hi = sem("turned_hi")
        sq_made = sem("sq_made")
        sq_folded = sem("sq_folded")
        on_made = sem("on_made")
        on_hi = sem("on_hi")
        heads_ready = sem("heads_ready")
        st_in = [sem(f"st_in{n}") for n in range(4)]
        st_out = [sem(f"st_out{n}") for n in range(4)]
        ps_out = sem("ps_out")
        merged = sem("merged")
        merged_hi = sem("merged_hi")
        merged_ready = sem("merged_ready")
        res_sq = sem("res_sq")
        sq_summed = sem("sq_summed")
        res_hi = sem("res_hi")
        res_ready = sem("res_ready")
        hid_hi = sem("hid_hi")
        hid_ready = sem("hid_ready")
        rstd_made = sem("rstd_made")
        y_made = sem("y_made")
        y_pool_made = sem("y_pool_made")
        y_out = sem("y_out")
        went_on = {eng.engine: sem(f"went_on_{n}") for n, eng in
                   enumerate((nc.sync, nc.gpsimd, nc.scalar, nc.vector))}

        Y_DVE = 6
        FIRST_UNITS = ((0, 0), (0, 1), (1, 0), (0, 2), (1, 1), (0, 3), (1, 2), (1, 3))
        FIRST_DONE = tuple(FIRST_UNITS.index((0, u)) + 1 for u in range(UNITS))

        LATE = fills(0, HG, HPAIRS, 0)

        block = ctx.enter_context(nc.Block())

        def was_read(eng, bank, phase, n, fill, apart=False):
            if apart:
                wait_apart(eng, free[bank], fills(bank, phase, n, fill) + 1)
            else:
                eng.wait_ge(free[bank], fills(bank, phase, n, fill) + 1)

        def slab_done(eng, m, par):
            eng.wait_ge(mm_done, 8 * m + (4 * par + 4))

        def slab_read(eng, m, par):
            eng.wait_ge(acc_free[par], m + 1)

        def wait_apart(eng, sem, value):
            eng.wait_ge(sem, value)
            if not isinstance(value, int):
                eng.sem_inc(went_on[eng.engine], 1)

        def level_bank(phase, level):
            bank, fill = ((0, 0), (2, 0), (3, 0), (0, 1), (1, 1), (0, 2), (1, 2), (0, 3))[level]
            return bank, fill + (1 if phase == GLA and bank == 0 else 0)

        STATES_FILL = (((2, 4), (3, 4)), ((0, 5), (1, 4)))
        V_FILL, K_FILL = (1, 1), (3, 2)

        def score_fill(phase, n):
            bank, fill = level_bank(phase, LEVELS - 1)
            return bank, phase, n, fill

        def after(m, par):
            return (m, 1) if par == 0 else (m + 1, 0)

        @block.sync
        def _(sp):
            sp.dma_start(vec[:], vectors).then_inc(vec_there, 16)
            x_tiles = x_t.rearrange("(k p) t -> p k t", p=P)
            for c in range(4):
                sp.dma_start(m_sb[:, 4 * c:4 * c + 4, :], x_tiles[:, 4 * c:4 * c + 4, :]).then_inc(x_in[c], 16)
            sp.dma_start(ones[:], ones_in).then_inc(ones_there, 16)

            def slab(m, par, weights, row, col):
                for half in range(2):
                    slot = 2 * par + half
                    if not isinstance(m, int) or m >= 1:
                        wait_apart(sp, lo_made, 8 * m + (4 * par + 2 * half + 2 - 8))
                    src = weights[bass.ds(row + half * (D // 2), D // 2), bass.ds(col, W2)]
                    sp.dma_start(raw[:, slot, :, :], src.rearrange("(k p) n -> p k n", p=P))\
                      .then_inc(raw_in[slot], 16)

            def gla_weights(h):
                m = M_GLA + 3 * h
                slab(m, 1, w_in, 0, C_KA + DKA * h)
                slab(m + 1, 0, w_in, 0, C_QA + DKA * h)
                slab(m + 1, 1, w_in, 0, C_VA + DVA * h)
                slab(m + 2, 0, w_in, 0, C_VA + W2 + DVA * h)
                slab(m + 2, 1, w_in, 0, C_RA + DVA * h)
                slab(m + 3, 0, w_in, 0, C_RA + W2 + DVA * h)

            slab(0, 0, w_in, 0, C_GR)
            sp.dma_start(eye[:], eye_in).then_inc(consts_in, 16)
            sp.dma_start(own[:], own_in).then_inc(consts_in, 16)
            sp.dma_start(masks_f, masks_in).then_inc(consts_in, 16)
            gla_weights(0)
            with sp.Fori(1, HA) as h:
                gla_weights(h)
            with sp.Fori(0, NS2) as n:
                slab(M_MA + n, 1, w_in, 0, C_MA + W2 * n)
                slab(M_MA + n + 1, 0, w_branch_a, 0, W2 * n)
            with sp.Fori(0, HPAIRS) as n:
                slab(M_HG + 2 * n, 1, w_in, 0, C_FB + W2 * n)
                slab(M_HG + 2 * n + 1, 0, w_in, 0, C_QB + W2 * n)
                slab(M_HG + 2 * n + 1, 1, w_in, 0, C_IB + W2 * n)
                slab(M_HG + 2 * n + 2, 0, w_in, 0, C_RB + W2 * n)
            with sp.Fori(0, NS2) as n:
                slab(M_MB + n, 1, w_in, 0, C_MB + W2 * n)
                slab(M_MB + n + 1, 0, w_branch_b, 0, W2 * n)
            with sp.Fori(0, NS2 // 2) as n:
                slab(M_OUT + n, 1, w_out, 0, 2 * W2 * n)
                slab(M_OUT + n + 1, 0, w_out, 0, 2 * W2 * n + W2)
            with sp.Fori(0, QUARTERS) as c:
                with sp.Fori(0, NS2 // 2) as n:
                    slab(M_UP + M_Q * c + n, 1, w_up, 0, 2 * W2 * n + D * c)
                    slab(M_UP + M_Q * c + n + 1, 0, w_up, 0, 2 * W2 * n + D * c + W2)
                with sp.Fori(0, NS2 // 2) as n:
                    slab(M_DOWN + M_Q * c + n, 1, w_down, D * c, 2 * W2 * n)
                    slab(M_DOWN + M_Q * c + n + 1, 0, w_down, D * c, 2 * W2 * n + W2)
            y_tiles = y_t.rearrange("(k p) t -> p k t", p=P)
            for c in (0, 1, 2, Y_DVE, 3, 4, Y_DVE + 1, 5):
                if c < Y_DVE:
                    sp.wait_ge(y_made, c + 1)
                else:
                    sp.wait_ge(y_pool_made, c - Y_DVE + 1)
                sp.dma_start(y_tiles[:, 2 * c:2 * c + 2, :], m_sb[:, 2 * c:2 * c + 2, :]).then_inc(y_out, 16)
            sp.wait_ge(y_out, 16 * (KT // 2))

        @block.gpsimd
        def _(pool):
            def own_rows(dst, src, b):
                return pool.tensor_scalar(dst, src, own[0:src.shape[0], b:b + 1], 1.0, ALU.mult, ALU.mult)

            def gate_weights(h):
                pool.dma_start(wg[:], w_gate2[:, bass.ds(DKA * h, DKA)]).then_inc(wg_in, 16)

            def gla_states(h, last=False):
                def load(b):
                    if not isinstance(h, int) or 2 * h + b // 4 > 0:
                        wait_apart(pool, st_out[b % 4], 16 * (2 * h + b // 4))
                    src = state_gla[b, bass.ds(h, 1)].rearrange("h (j p) v -> p (h j) v", p=P)
                    pool.dma_start(st_gla[b % 4], src).then_inc(st_in[b % 4], 16)

                def rows(b):
                    if b >= 2:
                        wait_apart(pool, full[3], fills(3, GLA, h, 4 + b - 2) + 1)
                    own_rows(k_own_parts[b % 2], k_parts.bitcast(F32), b).then_inc(k_own_made, 1)

                for b in range(4):
                    load(b)
                was_read(pool, 3, GLA, h, K_FILL[GLA], apart=True)
                rows(0)
                rows(1)
                for b in range(SB):
                    was_read(pool, 3, GLA, h, 4 + b, apart=True)
                    dst = gla_sample[b, bass.ds(h, 1)].rearrange("h (j p) v -> p (h j) v", p=P)
                    pool.dma_start(dst, st_gla[b % 4]).then_inc(st_out[b % 4], 16)
                    if b + 2 < SB:
                        rows(b + 2)
                    if 4 <= b + 3 < SB:
                        load(b + 3)
                if not last:
                    wait_apart(pool, full[1], fills(1, GLA, h, 0) + 1)
                    gate_weights(h + 1)
                was_read(pool, 3, GLA, h, 12, apart=True)
                dst = gla_prompt[bass.ds(h, 1)].rearrange("h (j p) v -> p (h j) v", p=P)
                pool.dma_start(dst, ps_gla).then_inc(ps_out, 16)

            def hgrn_states(n, first):
                if first:
                    pool.wait_ge(heads_ready, HA)
                for j in range(2):
                    wait_apart(pool, st_out[j], 16 * per(HG, n, 2, 1, 0))
                    src = state_hgrn[:, bass.ds(2 * n + j, 1)].rearrange("b h k v -> k (b h) v")
                    pool.dma_start(st_hg[:, j], src).then_inc(st_in[j], 16)
                was_read(pool, 3, HG, n, K_FILL[HG], apart=True)
                wait_apart(pool, full[3], fills(3, HG, n, 3) + 1)
                for c in range(4):
                    j, half = 1 - c // 2, c % 2
                    if c >= 2:
                        bank, fill = STATES_FILL[1][half]
                        wait_apart(pool, full[bank], fills(bank, HG, n, fill) + 1)
                    for b in range(4):
                        ins = own_rows(k_own[0:NSM, half, b * P:(b + 1) * P],
                                       k_tok[0:NSM, 2, j * P:(j + 1) * P], 4 * half + b)
                    ins.then_inc(k_own_made, 1)
                for j in (1, 0):
                    was_read(pool, (3, 1)[j], HG, n, 4, apart=True)
                    dst = hgrn_sample[:, bass.ds(2 * n + j, 1)].rearrange("b h k v -> k (b h) v")
                    pool.dma_start(dst, st_hg[:, j]).then_inc(st_out[j], 16)
                was_read(pool, 0, HG, n, 6, apart=True)
                pool.dma_start(hgrn_prompt[bass.ds(2 * n, 2)].rearrange("h k v -> k h v"), ps_hg)\
                    .then_inc(ps_out, 16)

            gate_weights(0)
            pool.wait_ge(consts_in, 16 * 3)
            pool.wait_ge(h_ready, 4)
            gla_states(0)
            with pool.Fori(1, HA - 1) as h:
                gla_states(h)
            gla_states(HA - 1, last=True)
            hgrn_states(0, True)
            with pool.Fori(1, HPAIRS) as n:
                hgrn_states(n, False)
            pool.wait_ge(heads_ready, HA + HPAIRS)
            for j in range(2):
                pool.wait_ge(st_out[j], 16 * per(HG, HPAIRS, 2, 1, 0))
            for j in range(2, 4):
                pool.wait_ge(st_out[j], 16 * 2 * HA)
            pool.wait_ge(ps_out, 16 * (HA + HPAIRS))
            pool.dma_start(x_res, x_t.rearrange("(k p) t -> p k t", p=P)).then_inc(x_res_in, 16)
            pool.wait_ge(rstd_made, 1)
            for c in range(Y_DVE, KT // 2):
                tiles = m_sb[:, 2 * c:2 * c + 2, :]
                pool.tensor_tensor(tiles, tiles, norm[:, 0:1, :].to_broadcast([P, 2, T]), ALU.mult)\
                    .then_inc(y_pool_made, 1)

        @block.tensor
        def _(pe):
            def unit(m, par, u, hi, lo, blocks=2):
                pe.wait_ge(lo_made, 8 * m + (4 * par + u + 1))
                if u == 0:
                    wait_from(pe, acc_free[par], m)
                for j in range(blocks):
                    for i in range(UK):
                        kt, cols = u * UK + i, slice(j * P, (j + 1) * P)
                        start, stop = kt == 0, kt == KT - 1
                        sums = acc[par][:, j, 0:T]
                        pe.matmul(sums, w_hi[:, u, i, cols], hi[:, kt, :], start=start, stop=False)
                        pe.matmul(sums, w_hi[:, u, i, cols], lo[:, kt, :], start=False, stop=False)
                        ins = pe.matmul(sums, w_lo[:, u, i, cols], hi[:, kt, :], start=False, stop=stop)
                ins.then_inc(mm_done, 1)

            def empty(bank, phase, n, fill):
                wait_from(pe, free[bank], fills(bank, phase, n, fill))

            def small(out, lhs, rhs, start=True, stop=True):
                return pe.matmul(out, lhs, rhs, start=start, stop=stop, skip_group_check=True)

            def scores(phase, n, level):
                pe.wait_ge(level_ready, per(phase, n, LEVELS, LEVELS, level + 1))
                first_bank, fill = level_bank(phase, level)
                heads = 2 if phase == HG else 1
                if level == 0:
                    for h in range(heads):
                        empty(h, phase, n, fill)
                else:
                    empty(first_bank, phase, n, fill)
                for h in range(heads):
                    keys = [h] if phase == HG else [0, 1]
                    bank = spare[h] if level == 0 else spare[first_bank]
                    at = NPR + NSM if level == 0 else 160 * h
                    todo = []
                    if level == 0:
                        todo += [(P, slice(tt * P, (tt + 1) * P), slice(tt * P, (tt + 1) * P), None, tt * P)
                                 for tt in range(2)]
                        todo += [(NSM, slice(NPR, T), slice(NPR, T), None, NPR)]
                    if level < 6:
                        todo += [(P, slice(tt * P, (tt + 1) * P), slice(tt * P, (tt + 1) * P), level, at + 64 * tt)
                                 for tt in range(2)]
                        if level < 3:
                            todo += [(NSM, slice(NPR, T), slice(NPR, T), level, at + P)]
                    elif level == 6:
                        todo += [(64, slice(tt * P, tt * P + 64), slice(tt * P + 64, tt * P + P), None, at + 64 * tt)
                                 for tt in range(2)]
                    else:
                        todo += [(P, slice(0, P), slice(P, NPR), None, at)]
                    for rows, s_at, t_at, lv, col in todo:
                        for j in keys:
                            qs = q[:, j, t_at] if lv is not None or level > 0 else q_raw[:, j, t_at]
                            if lv is not None:
                                qs = halves(qs, lv)[:, :, 1, :]
                            size = (t_at.stop - t_at.start) // (2 if lv is not None else 1)
                            ins = small(bank[0:rows, col:col + size], k[:, j, s_at], qs,
                                        j == keys[0], j == keys[-1])
                    if h == 0 and heads == 2 and level == 0:
                        ins.then_inc(full[0], 1)
                ins.then_inc(full[1 if phase == HG and level == 0 else first_bank], 1)

            def turn(src, phase, n, fill):
                for j in range(2):
                    empty(2 + j, phase, n, fill)
                    for tt, size in enumerate((P, P, NSM)):
                        ins = pe.transpose(spare[2 + j][0:size, tt * P:(tt + 1) * P],
                                           src[:, j, tt * P:tt * P + size], eye[:])
                    ins.then_inc(full[2 + j], 1)

            def gla_gate(h):
                pe.wait_ge(wg_in, 16 * (h + 1))
                for j in range(2):
                    empty(j, GLA, h, 0)
                    small(spare[j][:, 0:T], wg[:, j * P:(j + 1) * P], gr[:]).then_inc(full[j], 1)

            def gla_turn_v(h, c):
                slab_read(pe, M_GLA + 3 * h + 1 + c, 1 - c)
                turn(v_t, GLA, h, V_FILL[GLA] + c)

            def gla_turn_k(h):
                pe.wait_ge(k_final, h + 1)
                turn(k, GLA, h, K_FILL[GLA])

            def gla_sample_scores(h):
                was_read(pe, 3, GLA, h, V_FILL[GLA] + 1)
                was_read(pe, *score_fill(GLA, h))
                empty(1, GLA, h, 3)
                for v in range(4):
                    small(spare[1][:, v * NSM:(v + 1) * NSM], v_parts[:, v * P:(v + 1) * P].bitcast(F32),
                          sc[:, 0, 384:448], v == 0, False)

            def gla_state(h, b):
                pe.wait_ge(st_in[b % 4], 32 * h + 16 * (b // 4 + 1))
                for v in range(4):
                    for j in range(2):
                        at = v * NSM + b * SL
                        ins = small(spare[1][:, at:at + SL], st_gla[b % 4][:, j, v * P:(v + 1) * P],
                                    q[:, j, NPR + b * SL:NPR + (b + 1) * SL], False, b == SB - 1 and j == 1)
                if b == SB - 1:
                    ins.then_inc(full[1], 1)
                pe.wait_ge(k_own_made, per(GLA, h, 8, 4, b + 1))
                for j in range(2):
                    empty(2 + j, GLA, h, 4 + b)
                    for at in (j * P, DKA + j * P):
                        ins = small(spare[2 + j][:, :], k_own_parts[b % 2][:, at:at + P], v_parts, at < DKA, at >= DKA)
                    ins.then_inc(full[2 + j], 1)

            def prompt_out(out, phase, h, v):
                cols = slice(v * P, (v + 1) * P)
                small(out[:, 0:NPR], v_tok[phase][:, 0, cols], sc[:, h, 0:NPR], True, False)
                return small(out[:, P:NPR], v_tok[phase][:, 1, cols], sc[:, h, NPR:NPR + P], False, True)

            def gla_prompt_out(h, v):
                empty(0, GLA, h, 5 + v)
                prompt_out(spare[0], GLA, 0, v).then_inc(full[0], 1)

            def gla_squares(h):
                pe.wait_ge(sq_folded, h + 1)
                empty(0, GLA, h, 9)
                small(spare[0][:, 0:T], ones[:], sq[GLA][:, 0, :]).then_inc(full[0], 1)

            def gla_prompt_state(h):
                for j in range(2):
                    empty(2 + j, GLA, h, 12)
                    for tt in range(2):
                        ins = small(spare[2 + j][:, :], k_tok[:, tt, j * P:(j + 1) * P], v_tok[GLA][:, tt, :],
                                    tt == 0, tt == 1)
                    ins.then_inc(full[2 + j], 1)

            def gla_tail(h, slot):
                if slot < 3:
                    gla_state(h, 5 + slot)
                elif slot == 3:
                    gla_squares(h)
                else:
                    gla_prompt_state(h)

            def gla_head(h, tail):
                m = M_GLA + 3 * h
                if tail:
                    for u in range(UNITS):
                        unit(m, 1, u, a_hi, a_lo)
                        gla_tail(h - 1, u)
                for u in range(UNITS):
                    unit(m + 1, 0, u, a_hi, a_lo)
                    if tail and u == 0:
                        gla_tail(h - 1, 4)
                    if u == 1:
                        gla_gate(h)
                for u in range(UNITS):
                    unit(m + 1, 1, u, a_hi, a_lo)
                    if u > 0:
                        scores(GLA, h, u - 1)
                for u in range(UNITS):
                    unit(m + 2, 0, u, a_hi, a_lo)
                    scores(GLA, h, 3 + u)
                    if u == 2:
                        gla_turn_v(h, 0)
                for u in range(UNITS):
                    unit(m + 2, 1, u, a_hi, a_lo)
                    if u == 0:
                        scores(GLA, h, 7)
                    if u == 1:
                        gla_turn_v(h, 1)
                    if u == 2:
                        gla_turn_k(h)
                    if u == 3:
                        gla_sample_scores(h)
                        gla_state(h, 0)
                for u in range(UNITS):
                    unit(m + 3, 0, u, a_hi, a_lo)
                    gla_prompt_out(h, u)
                    gla_state(h, 1 + u)

            def hgrn_out(n, j):
                was_read(pe, 3, HG, n, V_FILL[HG])
                was_read(pe, *score_fill(HG, n))
                pe.wait_ge(st_in[j], 16 * per(HG, n, 2, 1, 1))
                empty(j, HG, n, 4 - j)
                out = spare[j]
                prompt_out(out, HG, j, j)
                small(out[:, NPR:T], v_tok[HG][0:NSM, 2, j * P:(j + 1) * P], sc[0:NSM, j, 384:448], False, False)
                for b in range(SB):
                    at = slice(NPR + b * SL, NPR + (b + 1) * SL)
                    ins = small(out[:, at], st_hg[:, j, b, :], q[:, j, at], False, b == SB - 1)
                ins.then_inc(full[j], 1)

            def hgrn_squares(n):
                for j in range(2):
                    was_read(pe, j, HG, n, 4 - j)
                    empty(2 + j, HG, n, 3)
                    small(spare[2 + j][:, 0:T], ones[:], sq[HG][:, j, :]).then_inc(full[2 + j], 1)

            def hgrn_prompt_states(n):
                empty(0, HG, n, 6)
                for j in range(2):
                    for tt in range(2):
                        cols = slice(j * P, (j + 1) * P)
                        ins = small(spare[0][:, cols], k_tok[:, tt, cols], v_tok[HG][:, tt, cols], tt == 0, tt == 1)
                ins.then_inc(full[0], 1)

            def hgrn_states(n, j):
                for half in range(2):
                    bank, fill = STATES_FILL[j][half]
                    pe.wait_ge(k_own_made, per(HG, n, 8, 4, 2 * (1 - j) + half + 1))
                    empty(bank, HG, n, fill)
                    for b in range(4):
                        ins = small(spare[bank][:, b * P:(b + 1) * P], k_own[0:NSM, half, b * P:(b + 1) * P],
                                    v_tok[HG][0:NSM, 2, j * P:(j + 1) * P])
                    ins.then_inc(full[bank], 1)

            def hgrn_tail(n, slot):
                if slot == 0:
                    scores(HG, n, 7)
                elif slot == 1:
                    pe.wait_ge(k_final, HA + 1 + n)
                    turn(k, HG, n, K_FILL[HG])
                    hgrn_out(n, 0)
                elif slot == 2:
                    hgrn_out(n, 1)
                elif slot == 3:
                    hgrn_squares(n)
                elif slot in (5, 6):
                    hgrn_states(n, 6 - slot)
                elif slot == 7:
                    hgrn_prompt_states(n)

            def hgrn_pair(n, tail):
                m = M_HG + 2 * n
                for u in range(UNITS):
                    unit(m, 1, u, a_hi, a_lo)
                    if tail:
                        hgrn_tail(n - 1, u)
                for u in range(UNITS):
                    unit(m + 1, 0, u, a_hi, a_lo)
                    if tail:
                        hgrn_tail(n - 1, 4 + u)
                for u in range(UNITS):
                    unit(m + 1, 1, u, a_hi, a_lo)
                    if u > 0:
                        scores(HG, n, u - 1)
                for u in range(UNITS):
                    unit(m + 2, 0, u, a_hi, a_lo)
                    scores(HG, n, 3 + u)
                    if u == 2:
                        slab_read(pe, m + 1, 1)
                        turn(v_t, HG, n, V_FILL[HG])

            def merge_a(n, tail):
                for u in range(UNITS):
                    unit(M_MA + n, 1, u, a_hi, a_lo)
                    if tail:
                        gla_tail(HA - 1, u)
                for u in range(UNITS):
                    pe.wait_ge(heads_ready, u + 1)
                    unit(M_MA + n + 1, 0, u, b_hi, b_lo)
                    if tail and u == 0:
                        gla_tail(HA - 1, 4)

            def merge_b(n, tail):
                for u in range(UNITS):
                    unit(M_MB + n, 1, u, a_hi, a_lo)
                    if tail:
                        hgrn_tail(HPAIRS - 1, u)
                for u in range(UNITS):
                    pe.wait_ge(heads_ready, HA + 2 * (u + 1))
                    unit(M_MB + n + 1, 0, u, b_hi, b_lo)
                    if tail:
                        hgrn_tail(HPAIRS - 1, 4 + u)

            def sum_squares(value, fill):
                pe.wait_ge(sq_summed, value)
                pe.wait_ge(free[0], fill)
                for j in range(2):
                    ins = small(spare[0][:, 0:T], ones[:], sq_sum[:, j, :], j == 0, j == 1)
                ins.then_inc(full[0], 1)

            def up_pair(n, c, first=False):
                for u in range(UNITS):
                    if first:
                        pe.wait_ge(res_ready, 2 * (u + 1))
                    unit(M_UP + M_Q * c + n, 1, u, b_hi, b_lo)
                    if first and u == 2:
                        sum_squares(NS2 + 1, LATE)
                for u in range(UNITS):
                    unit(M_UP + M_Q * c + n + 1, 0, u, b_hi, b_lo)

            def down(c):
                with pe.Fori(0, NS2 // 2) as n:
                    for u in range(UNITS):
                        pe.wait_ge(hid_ready, c * NS2 + 2 * (u + 1) + 1)
                        unit(M_DOWN + M_Q * c + n, 1, u, a_hi, a_lo)
                    for u in range(UNITS):
                        unit(M_DOWN + M_Q * c + n + 1, 0, u, a_hi, a_lo)

            pe.wait_ge(ones_there, 16)
            pe.wait_ge(sq_in_added, 4)
            for i in range(2):
                ins = small(spare[0][:, 0:T], ones[:], sq_in[0][:, i, :], i == 0, i == 1)
            ins.then_inc(full[0], 1)
            for par, u in FIRST_UNITS:
                pe.wait_ge(h_ready, u + 1)
                unit(0, par, u, a_hi, a_lo, blocks=1 + par)
            pe.wait_ge(consts_in, 16 * 3)
            slab_read(pe, 0, 0)
            gla_head(0, False)
            with pe.Fori(1, HA) as h:
                gla_head(h, True)
            merge_a(0, True)
            with pe.Fori(1, NS2) as n:
                merge_a(n, False)
            hgrn_pair(0, False)
            with pe.Fori(1, HPAIRS) as n:
                hgrn_pair(n, True)
            merge_b(0, True)
            with pe.Fori(1, NS2) as n:
                merge_b(n, False)
            with pe.Fori(0, NS2 // 2) as n:
                for u in range(UNITS):
                    pe.wait_ge(merged_ready, u + 1)
                    unit(M_OUT + n, 1, u, a_hi, a_lo)
                for u in range(UNITS):
                    unit(M_OUT + n + 1, 0, u, a_hi, a_lo)
            up_pair(0, 0, first=True)
            with pe.Fori(1, NS2 // 2) as n:
                up_pair(n, 0)
            down(0)
            with pe.Fori(1, QUARTERS) as c:
                with pe.Fori(0, NS2 // 2) as n:
                    up_pair(n, c)
                down(c)
            sum_squares(2 * NS2 + 2, LATE + 1)

        @block.scalar
        def _(act):
            me = Tally(act, act_self)

            def split(m, par, u):
                slot = 2 * par + u // 2
                if isinstance(m, int) and m == 0:
                    if par == 1:
                        act.wait_ge(mm_done, FIRST_DONE[u])
                else:
                    act.wait_ge(mm_done, 8 * m + (4 * par + u - 3))
                act.wait_ge(raw_in[slot], 16 * (m + 1))
                act.activation(w_hi[:, u, :, :], raw[:, slot, (u % 2) * UK:(u % 2 + 1) * UK, :], ACT.Copy)\
                   .then_inc(hi_made, 1)

            def filled(bank, phase, n, fill):
                act.wait_ge(full[bank], fills(bank, phase, n, fill) + 1)

            def slab_out(m, par, out, func, scale=1.0, release=True):
                slab_done(act, m, par)
                ins = act.activation(out, acc[par][:, :, 0:T], func, scale=scale)
                ins.then_inc(acc_free[par] if release else sig_made, 1)

            def from_turned(dst, at, phase, n, fill):
                for j in range(2):
                    filled(2 + j, phase, n, fill)
                    cols = slice(at + j * P, at + (j + 1) * P)
                    act.activation(dst[:, 0:2, cols], spare[2 + j][:, 0:NPR].rearrange("p (a b) -> p a b", b=P),
                                   ACT.Copy)
                    sample = spare[2 + j][0:NSM, NPR:NPR + P]
                    if phase == HG:
                        act.activation(dst[0:NSM, 2, cols], sample, ACT.Copy).then_inc(free[2 + j], 1)
                        continue
                    if dst is k_tok:
                        act.activation(k_parts[NSM:2 * NSM, cols], sample, ACT.Copy)
                    hi = k_parts if dst is k_tok else v_parts
                    act.activation(hi[0:NSM, cols], sample, ACT.Copy).then_inc(turned_hi, 1)

            def inverse_root(mean_square, out, log):
                me.link(act.activation(log, mean_square, ACT.Ln), wait_apart)
                act.activation(out, log, ACT.Exp, scale=-0.5).then_inc(guess_made, 1)

            def head_hi(phase, n, tiles):
                act.wait_ge(on_made, per(phase, n, 1, 1, 1))
                act.activation(b_hi[:, tiles, :], o_sb[phase], ACT.Copy).then_inc(on_hi, 1)

            def gla_tail(h, slot):
                if slot == 2:
                    filled(1, GLA, h, 3)
                    ins = act.activation(o_sb[GLA][:, :, NPR:T],
                                         spare[1][:, 0:4 * NSM].rearrange("p (v t) -> p v t", v=4), ACT.Copy)
                    ins.then_inc(free[1], 1)
                    was_read(act, 1, GLA, h, 3)
                    filled(3, GLA, h, 11)
                    act.activation(sq[GLA], o_sb[GLA], ACT.Square).then_inc(sq_made, 1)
                if slot == 3:
                    was_read(act, 0, GLA, h, 9)
                    inverse_root(norm[:, 0, :], guess, guess)
                if slot == 4:
                    wait_from(act, ps_out, 16 * h)
                    for j in range(2):
                        filled(2 + j, GLA, h, 12)
                        act.activation(ps_gla[:, j, :], spare[2 + j][:, :], ACT.Copy).then_inc(free[2 + j], 1)

            def gla_gate(h):
                wait_from(act, level_ready, LEVELS * h)
                for j in range(2):
                    filled(j, GLA, h, 0)
                    act.activation(g[:, j, :], spare[j][:, 0:T], ACT.Identity,
                                   bias=vec[:, bass.ds(2 * h + (V_BG + j), 1)]).then_inc(free[j], 1)
                was_read(act, 1, GLA, h, 0)
                me.link(act.activation(q_raw, g, ACT.Abs))
                me.link(act.activation(q_raw, q_raw, ACT.Exp, scale=-1.0))
                act.activation(q_raw, q_raw, ACT.Ln, bias=1.0).then_inc(soft_made, 1)
                act.wait_ge(log_made, h + 1)
                act.activation(g, g, ACT.Exp, scale=1.0 / GATE_NORM).then_inc(g_made, 1)

            def gla_head(h, tail):
                m = M_GLA + 3 * h
                for u in range(UNITS):
                    split(m + 1, 0, u)
                    if tail:
                        gla_tail(h - 1, u)
                slab_out(m, 1, k, ACT.Copy)
                for u in range(UNITS):
                    split(m + 1, 1, u)
                    if tail and u == 0:
                        gla_tail(h - 1, 4)
                    if u == 1:
                        gla_gate(h)
                slab_out(m + 1, 0, q_raw, ACT.Copy, scale=DKA ** -0.5)
                for u in range(UNITS):
                    split(m + 2, 0, u)
                    if tail and u == 1:
                        head_hi(GLA, h - 1, bass.ds(4 * h - 4, 4))
                wait_from(act, norm_used, h)
                slab_out(m + 1, 1, v_t, ACT.Copy)
                for u in range(UNITS):
                    split(m + 2, 1, u)
                    if u == 2:
                        from_turned(v_tok[GLA], 0, GLA, h, V_FILL[GLA])
                slab_out(m + 2, 0, v_t, ACT.Copy)
                for u in range(UNITS):
                    split(m + 3, 0, u)
                    if u == 1:
                        from_turned(v_tok[GLA], 256, GLA, h, V_FILL[GLA] + 1)
                    if u == 2:
                        from_turned(k_tok, 0, GLA, h, K_FILL[GLA])
                wait_from(act, heads_ready, h)
                slab_out(m + 2, 1, r_sb[GLA][:, 0:2, :], ACT.Sigmoid, release=False)
                for u in range(UNITS):
                    split(m + 3, 1, u)
                    filled(0, GLA, h, 5 + u)
                    act.activation(o_sb[GLA][:, u, 0:NPR], spare[0][:, 0:NPR], ACT.Copy).then_inc(free[0], 1)
                slab_out(m + 3, 0, r_sb[GLA][:, 2:4, :], ACT.Sigmoid, release=False)

            def hgrn_tail(n, slot):
                if slot == 1:
                    from_turned(k_tok, 0, HG, n, K_FILL[HG])
                if slot in (1, 2):
                    j = slot - 1
                    filled(j, HG, n, 4 - j)
                    act.activation(o_sb[HG][:, j, :], spare[j][:, 0:T], ACT.Copy)
                    act.activation(sq[HG][:, j, :], spare[j][:, 0:T], ACT.Square).then_inc(free[j], 1)
                if slot == 4:
                    was_read(act, 3, HG, n, 3)
                    filled(3, HG, n, K_FILL[HG])
                    inverse_root(norm, pair_guess(n), k)
                if slot == 7:
                    act.wait_ge(ps_out, 16 * per(HG, n, 1, 1, 0))
                    filled(0, HG, n, 6)
                    act.activation(ps_hg, spare[0][:, 0:2 * P].rearrange("p (j v) -> p j v", j=2), ACT.Copy)\
                       .then_inc(free[0], 1)

            def hgrn_pair(n, tail):
                m = M_HG + 2 * n
                for u in range(UNITS):
                    split(m + 1, 0, u)
                    if tail:
                        hgrn_tail(n - 1, u)
                act.wait_ge(level_ready, per(HG, n, LEVELS, LEVELS, 0))
                slab_out(m, 1, g, ACT.Sigmoid)
                if tail:
                    hgrn_tail(n - 1, 4)
                for u in range(UNITS):
                    split(m + 1, 1, u)
                    if tail and u > 0:
                        hgrn_tail(n - 1, 4 + u)
                act.wait_ge(norm_used, per(HG, n, 1, 1, 0))
                slab_out(m + 1, 0, v_t, ACT.Sigmoid, release=False)
                for u in range(UNITS):
                    split(m + 2, 0, u)
                    if tail and u == 1:
                        head_hi(HG, n - 1, bass.ds(2 * n - 2, 2))
                slab_read(act, m + 1, 0)
                slab_out(m + 1, 1, v_t, ACT.Copy)
                for u in range(UNITS):
                    split(m + 2, 1, u)
                    if u == 2:
                        from_turned(v_tok[HG], 0, HG, n, V_FILL[HG])
                act.wait_ge(heads_ready, per(HG, n, 1, 1, 0))
                slab_out(m + 2, 0, r_sb[HG], ACT.Sigmoid, release=False)

            def merged_to_hi(c):
                act.wait_ge(merged, 2 * c + 2)
                act.activation(a_hi[:, 4 * c:4 * c + 4, :], m_sb[:, 4 * c:4 * c + 4, :], ACT.Copy)\
                   .then_inc(merged_hi, 1)

            def merge_a(n, tail):
                for u in range(UNITS):
                    split(M_MA + n + 1, 0, u)
                    if tail:
                        gla_tail(HA - 1, u)
                slab_read(act, M_MA + n, 0)
                slab_out(M_MA + n, 1, gate, ACT.Sigmoid)
                for u in range(UNITS):
                    split(M_MA + n + 1, 1, u)
                    if tail and u == 0:
                        gla_tail(HA - 1, 4)
                    if tail and u == 0:
                        head_hi(GLA, HA - 1, bass.ds(4 * HA - 4, 4))

            def merge_b(n, tail, last=False):
                for u in range(UNITS):
                    split(M_MB + n + 1, 0, u)
                    if tail:
                        hgrn_tail(HPAIRS - 1, u)
                if tail:
                    hgrn_tail(HPAIRS - 1, 4)
                    act.wait_ge(guess_made, HA + HPAIRS + 1)
                wait_from(act, merged, n)
                slab_out(M_MB + n, 1, gate, ACT.Sigmoid)
                for u in range(UNITS):
                    split(M_MB + n + 1, 1, u)
                    if tail and u > 0:
                        hgrn_tail(HPAIRS - 1, 4 + u)
                    if tail and u == 0:
                        head_hi(HG, HPAIRS - 1, bass.ds(2 * HPAIRS - 2, 2))
                    if last and u < UNITS - 1:
                        merged_to_hi(u)

            def squares(m, par, tile, index, clears):
                wait_apart(act, acc_free[par], m + 1)
                wait_apart(act, sq_summed, index + clears)
                act.activation(sq_new, m_sb[:, bass.ds(tile, 2), :], ACT.Square).then_inc(res_sq, 1)

            def out_end(m, par, index):
                slab_read(act, m, par)
                for j in range(2):
                    ins = act.activation(b_hi[:, bass.ds(2 * index + j, 1), :], m_sb[:, bass.ds(2 * index + j, 1), :],
                                         ACT.Copy, scale=vec[:, bass.ds(2 * index + (V_MLP + j), 1)])
                ins.then_inc(res_hi, 1)
                squares(m, par, 2 * index, index, 1)

            def up_end(m, par, index, c):
                act.wait_ge(hid_ready, c * NS2 + index + 1)
                slab_read(act, m, par)
                me.link(act.activation(hid_f, hid_t, ACT.Square))
                act.activation(a_hi[:, bass.ds(2 * index, 2), :], hid_f, ACT.Copy).then_inc(hid_hi, 1)

            def up_pair(n, c, first=False):
                m = M_UP + M_Q * c + n
                for u in range(UNITS):
                    split(m + 1, 0, u)
                    if first and u == 2:
                        act.wait_ge(free[0], LATE + 1)
                        inverse_root(norm[:, 0, :], guess, guess)
                up_end(m, 1, 2 * n, c)
                for u in range(UNITS):
                    split(m + 1, 1, u)
                up_end(m + 1, 0, 2 * n + 1, c)

            def up(c):
                with me.loop(0, NS2 // 2, 2) as n:
                    up_pair(n, c)

            def down(n, c, last, end):
                m = M_DOWN + M_Q * c + n
                for u in range(UNITS):
                    split(m + 1, 0, u)
                if last:
                    squares(m, 1, 4 * n, 2 * n + NS2, 2)
                for u in range(UNITS):
                    if not end:
                        split(m + 1, 1, u)
                if last:
                    squares(m + 1, 0, 4 * n + 2, 2 * n + (NS2 + 1), 2)

            for c in range(4):
                act.wait_ge(x_in[c], 16)
                if c == 3:
                    act.wait_ge(sq_in_added, 1)
                act.activation(sq_in[(0, 1, 2, 1)[c]], m_sb[:, 4 * c:4 * c + 4, :], ACT.Square)\
                   .then_inc(sq_in_made, 1)
            for u in range(UNITS):
                if u == 2:
                    act.wait_ge(free[0], 1)
                    inverse_root(norm[:, 0, :], guess, guess)
                    act.wait_ge(lb_max, 1)
                    act.activation(soft[:, 0:2, :], soft[:, 0:2, :], ACT.Exp).then_inc(lb_exp, 1)
                split(0, 0, u)
            for c in range(UNITS):
                act.wait_ge(h_made, c + 1)
                act.activation(a_hi[:, 4 * c:4 * c + 4, :], m_sb[:, 4 * c:4 * c + 4, :], ACT.Copy).then_inc(h_hi, 1)
                if c > 0:
                    split(0, 1, c - 1)
            split(0, 1, UNITS - 1)
            act.wait_ge(mm_done, FIRST_DONE[UNITS - 1])
            act.activation(gr[:], acc[0][0:RANK, 0, 0:T], ACT.Copy).then_inc(acc_free[0], 1)
            gla_head(0, False)
            with me.loop(1, HA, 3) as h:
                gla_head(h, True)
            merge_a(0, True)
            with act.Fori(1, NS2) as n:
                merge_a(n, False)
            hgrn_pair(0, False)
            with me.loop(1, HPAIRS, 1) as n:
                hgrn_pair(n, True)
            merge_b(0, True)
            with act.Fori(1, NS2 - 1) as n:
                merge_b(n, False)
            merge_b(NS2 - 1, False, last=True)
            merged_to_hi(UNITS - 1)
            with act.Fori(0, NS2 // 2) as n:
                for u in range(UNITS):
                    split(M_OUT + n + 1, 0, u)
                out_end(M_OUT + n, 1, 2 * n)
                for u in range(UNITS):
                    split(M_OUT + n + 1, 1, u)
                out_end(M_OUT + n + 1, 0, 2 * n + 1)
            up_pair(0, 0, first=True)
            with me.loop(1, NS2 // 2, 2) as n:
                up_pair(n, 0)
            with act.Fori(0, NS2 // 2) as n:
                down(n, 0, False, False)
            with me.loop(1, QUARTERS - 1, NS2) as c:
                up(c)
                with act.Fori(0, NS2 // 2) as n:
                    down(n, c, False, False)
            up(QUARTERS - 1)
            with act.Fori(0, NS2 // 2 - 1) as n:
                down(n, QUARTERS - 1, True, False)
            down(NS2 // 2 - 1, QUARTERS - 1, True, True)
            act.wait_ge(free[0], LATE + 2)
            inverse_root(norm[:, 0, :], guess, guess)

        @block.vector
        def _(dve):
            me = Tally(dve, dve_self)

            def split(m, par, u):
                slot = 2 * par + u // 2
                if isinstance(m, int) and m == 0:
                    if par == 1:
                        dve.wait_ge(mm_done, FIRST_DONE[u])
                else:
                    dve.wait_ge(mm_done, 8 * m + (4 * par + u - 3))
                dve.wait_ge(hi_made, 8 * m + (4 * par + u + 1))
                dve.tensor_tensor(w_lo[:, u, :, :], raw[:, slot, (u % 2) * UK:(u % 2 + 1) * UK, :],
                                  w_hi[:, u, :, :].bitcast(F32), ALU.subtract).then_inc(lo_made, 1)

            def filled(bank, phase, n, fill):
                dve.wait_ge(full[bank], fills(bank, phase, n, fill) + 1)

            def mean(out, bank, count):
                return dve.tensor_scalar(out, spare[bank][:, 0:T], 1.0 / count, EPS, ALU.mult, ALU.add)

            def block_decays():
                for level in range(1, LEVELS):
                    n = TOT_N[level]
                    pairs = tot(level - 1)[:, :, 0:2 * n].rearrange("p j (n h) -> p j n h", h=2)
                    me.link(dve.tensor_tensor(tot(level), pairs[:, :, :, 0], pairs[:, :, :, 1], ALU.mult))

            def level(phase, n, lv):
                heads = 2 if phase == HG else 1
                bank, fill = level_bank(phase, lv)
                for h in range(heads):
                    src = spare[h] if lv == 0 else spare[bank]
                    if lv == 0 or h == 0:
                        at = h if lv == 0 else bank
                        wait_apart(dve, full[at], fills(at, phase, n, fill) + 1)
                    at = T if lv == 0 else 160 * h
                    if lv == 0:
                        for rows, col, to in ((P, 0, 0), (P, P, NPR), (NSM, NPR, NPR + P)):
                            ins = dve.copy_predicated(sc[0:rows, h, to:to + rows], masks[0:rows, 0:rows],
                                                      src[0:rows, col:col + rows])
                        me.link(ins, wait_apart)
                    if lv < 6:
                        mask = masks[:, P + 64 * lv:P + 64 * (lv + 1)]
                        for tt, (rows, size) in enumerate(((P, 64), (P, 64), (NSM, 32))[:3 if lv < 3 else 2]):
                            to = (0, NPR, NPR + P)[tt]
                            out = halves(sc[0:rows, h, to:to + 2 * size], lv)[:, :, 1, :]
                            ins = dve.copy_predicated(
                                out, mask[0:rows, 0:size].rearrange("p (n b) -> p n b", b=1 << lv),
                                src[0:rows, at + 64 * tt:at + 64 * tt + size]
                                .rearrange("p (n b) -> p n b", b=1 << lv))
                    elif lv == 6:
                        for tt in range(2):
                            ins = dve.tensor_copy(sc[0:64, h, NPR * tt + 64:NPR * tt + P],
                                                  src[0:64, at + 64 * tt:at + 64 * (tt + 1)])
                    else:
                        ins = dve.tensor_copy(sc[:, h, P:NPR], src[:, at:at + P])
                    if lv == 0 and heads == 2:
                        ins.then_inc(free[h], 1)
                if not (lv == 0 and heads == 2):
                    ins.then_inc(free[bank], 1)
                end = T if lv < 3 else NPR
                pairs = tot(lv)[:, :, 0:end >> lv].rearrange("p j (n h) -> p j n h", h=2)
                shape = [P, 2, end >> (lv + 1), 1 << lv]
                second = halves(q[:, :, 0:end], lv)[:, :, :, 1, :]
                first = halves(k[:, :, 0:end], lv)[:, :, :, 0, :]
                if lv < LEVELS - 1:
                    dve.tensor_tensor(second, second, pairs[:, :, :, 0:1].to_broadcast(shape), ALU.mult)
                dve.tensor_tensor(first, first, pairs[:, :, :, 1:2].to_broadcast(shape), ALU.mult)\
                   .then_inc(level_ready if lv < LEVELS - 1 else k_final, 1)

            def refine(mean_square, first, guesses):
                dve.wait_ge(guess_made, guesses)
                me.link(dve.tensor_tensor(mean_square, mean_square, first, ALU.mult))
                me.link(dve.scalar_tensor_tensor(out=mean_square, in0=mean_square, scalar=-0.5, in1=first,
                                                 op0=ALU.mult, op1=ALU.mult))
                me.link(dve.scalar_tensor_tensor(out=mean_square, in0=mean_square, scalar=1.5, in1=first,
                                                 op0=ALU.add, op1=ALU.mult))

            def head_norm(phase, n):
                used = norm[:, 0, :] if phase == GLA else norm
                refine(used, guess if phase == GLA else pair_guess(n).bitcast(F32), per(phase, n, 1, 1, 2))
                o = o_sb[phase]
                if phase == GLA:
                    for v in range(4):
                        ins = dve.scalar_tensor_tensor(out=o[:, v, :], in0=o[:, v, :], in1=used,
                                                       scalar=vec[:, V_GA + v:V_GA + v + 1], op0=ALU.mult,
                                                       op1=ALU.mult)
                else:
                    ins = dve.scalar_tensor_tensor(out=o, in0=o, scalar=vec[:, V_GB:V_GB + 1], in1=used,
                                                   op0=ALU.mult, op1=ALU.mult)
                ins.then_inc(norm_used, 1)

            def head_gate(phase, n):
                dve.wait_ge(norm_used, per(phase, n, 1, 1, 1))
                if phase == GLA:
                    slab_read(dve, M_GLA + 3 * n + 3, 0)
                else:
                    slab_read(dve, M_HG + 2 * n + 2, 0)
                o = o_sb[phase]
                dve.tensor_tensor(o, o, r_sb[phase], ALU.mult).then_inc(on_made, 1)

            def head_lo(phase, n, tiles):
                dve.wait_ge(on_hi, per(phase, n, 1, 1, 1))
                dve.tensor_tensor(b_lo[:, tiles, :], o_sb[phase], b_hi[:, tiles, :].bitcast(F32), ALU.subtract)\
                   .then_inc(heads_ready, 1)

            def swish(m, par, out, sig, sig_count):
                dve.wait_ge(sig_made, sig_count)
                dve.tensor_tensor(out, acc[par][:, :, 0:T], sig, ALU.mult).then_inc(acc_free[par], 1)

            def turned_lo(h, turn):
                for j in range(2):
                    dve.wait_ge(turned_hi, per(GLA, h, 6, 0, 2 * turn + j + 1))
                    sample = spare[2 + j][0:NSM, NPR:NPR + P]
                    if turn < 2:
                        at = slice(turn * 256 + j * P, turn * 256 + (j + 1) * P)
                        ins = dve.tensor_tensor(v_parts[NSM:2 * NSM, at], sample,
                                                v_parts[0:NSM, at].bitcast(F32), ALU.subtract)
                    else:
                        at, to = slice(j * P, (j + 1) * P), slice(DKA + j * P, DKA + (j + 1) * P)
                        for rows in (slice(0, NSM), slice(NSM, 2 * NSM)):
                            ins = dve.tensor_tensor(k_parts[rows, to], sample,
                                                    k_parts[0:NSM, at].bitcast(F32), ALU.subtract)
                    ins.then_inc(free[2 + j], 1)

            def gla_state(h, b):
                for j in range(2):
                    filled(2 + j, GLA, h, 4 + b)
                    st = st_gla[b % 4][:, j, :]
                    dve.scalar_tensor_tensor(out=st, in0=st, scalar=own_tot(j, b), in1=spare[2 + j][:, :],
                                             op0=ALU.mult, op1=ALU.add).then_inc(free[2 + j], 1)

            def gla_tail(h, slot):
                if slot < 3:
                    gla_state(h, 5 + slot)
                if slot == 2:
                    dve.wait_ge(sq_made, h + 1)
                    me.link(dve.tensor_tensor(sq[GLA][:, 0:2, :], sq[GLA][:, 0:2, :], sq[GLA][:, 2:4, :], ALU.add))
                    dve.tensor_tensor(sq[GLA][:, 0, :], sq[GLA][:, 0, :], sq[GLA][:, 1, :], ALU.add)\
                       .then_inc(sq_folded, 1)
                if slot == 3:
                    filled(0, GLA, h, 9)
                    mean(norm[:, 0, :], 0, DVA).then_inc(free[0], 1)
                if slot == 4:
                    head_norm(GLA, h)

            def gla_head(h, tail):
                m = M_GLA + 3 * h
                for u in range(UNITS):
                    split(m + 1, 0, u)
                    if tail:
                        gla_tail(h - 1, u)
                for u in range(UNITS):
                    split(m + 1, 1, u)
                    if tail and u == 0:
                        gla_tail(h - 1, 4)
                    if u == 1:
                        dve.wait_ge(soft_made, h + 1)
                        dve.scalar_tensor_tensor(out=g, in0=g, scalar=0.0, in1=q_raw, op0=ALU.min,
                                                 op1=ALU.subtract).then_inc(log_made, 1)
                    if u == 2:
                        dve.wait_ge(g_made, h + 1)
                        block_decays()
                slab_read(dve, m + 1, 0)
                dve.tensor_tensor(q, q_raw, g, ALU.mult).then_inc(level_ready, 1)
                for u in range(UNITS):
                    split(m + 2, 0, u)
                    if tail and u == 0:
                        head_gate(GLA, h - 1)
                    if u > 0:
                        level(GLA, h, u - 1)
                    if tail and u == 2:
                        head_lo(GLA, h - 1, bass.ds(4 * h - 4, 4))
                wait_apart(dve, level_ready, per(GLA, h, LEVELS, LEVELS, 4))
                dve.tensor_copy(sc[NSM:2 * NSM, 0, 384:448], sc[0:NSM, 0, 384:448])
                for u in range(UNITS):
                    split(m + 2, 1, u)
                    level(GLA, h, 3 + u)
                    if u == 2:
                        turned_lo(h, 0)
                for u in range(UNITS):
                    split(m + 3, 0, u)
                    if u == 0:
                        level(GLA, h, 7)
                    if u in (1, 2):
                        turned_lo(h, u)
                    if u == 3:
                        gla_state(h, 0)
                swish(m + 2, 1, r_sb[GLA][:, 0:2, :], r_sb[GLA][:, 0:2, :], 2 * h + 1)
                for u in range(UNITS):
                    split(m + 3, 1, u)
                    gla_state(h, 1 + u)
                swish(m + 3, 0, r_sb[GLA][:, 2:4, :], r_sb[GLA][:, 2:4, :], 2 * h + 2)

            def keep_own_decays():
                at = TOT_AT[3] + NPR // SL
                me.link(dve.tensor_copy(own_decays[:], tots[:, :, at:at + SB]))

            def hgrn_tail(n, slot):
                if slot == 0:
                    level(HG, n, 7)
                if slot == 3:
                    for j in range(2):
                        filled(2 + j, HG, n, 3)
                        mean(norm[:, j, :], 2 + j, P).then_inc(free[2 + j], 1)
                if slot == 4:
                    head_norm(HG, n)

            def hgrn_states(n, j):
                for half in range(2):
                    bank, fill = STATES_FILL[j][half]
                    filled(bank, HG, n, fill)
                    for b in range(4):
                        st, at = st_hg[:, j, 4 * half + b, :], 4 * half + b
                        ins = dve.scalar_tensor_tensor(out=st, in0=st, scalar=own_decays[:, j, at:at + 1],
                                                       in1=spare[bank][:, b * P:(b + 1) * P],
                                                       op0=ALU.mult, op1=ALU.add)
                    ins.then_inc(free[bank], 1)

            def hgrn_pair(n, tail):
                m = M_HG + 2 * n
                for u in range(UNITS):
                    split(m + 1, 0, u)
                    if tail:
                        hgrn_tail(n - 1, u)
                dve.wait_ge(full[3], fills(3, HG, n - 1, K_FILL[HG]) + 1 if tail
                            else fills(3, GLA, HA - 1, K_FILL[GLA]) + 1)
                slab_read(dve, m, 1)
                for j in range(2):
                    ins = dve.tensor_scalar(g[:, j, :], g[:, j, :], one_lb[:, bass.ds(2 * n + j, 1)],
                                            lb[:, bass.ds(2 * n + j, 1)], ALU.mult, ALU.add)
                me.link(ins)
                for u in range(UNITS):
                    split(m + 1, 1, u)
                    if tail:
                        hgrn_tail(n - 1, 4 + u)
                    if u == 0:
                        dve.tensor_scalar(k, g, -1.0, 1.0, ALU.mult, ALU.add)
                    if u == 1:
                        if tail:
                            keep_own_decays()
                        block_decays()
                    if tail and u == 2:
                        hgrn_states(n - 1, 1)
                swish(m + 1, 0, q_raw, v_t, per(HG, n, 2, 2, 1))
                slab_read(dve, m + 1, 0)
                dve.tensor_tensor(q, q_raw, g, ALU.mult).then_inc(level_ready, 1)
                if tail:
                    hgrn_states(n - 1, 0)
                for u in range(UNITS):
                    split(m + 2, 0, u)
                    if tail and u == 0:
                        head_gate(HG, n - 1)
                    if u > 0:
                        level(HG, n, u - 1)
                    if tail and u == 2:
                        head_lo(HG, n - 1, bass.ds(2 * n - 2, 2))
                for u in range(UNITS):
                    split(m + 2, 1, u)
                    level(HG, n, 3 + u)
                swish(m + 2, 0, r_sb[HG], r_sb[HG], per(HG, n, 2, 2, 2))

            def merge_a(n, tail):
                for u in range(UNITS):
                    split(M_MA + n + 1, 0, u)
                    if tail:
                        gla_tail(HA - 1, u)
                if tail:
                    gla_tail(HA - 1, 4)
                    head_gate(GLA, HA - 1)
                for u in range(UNITS):
                    split(M_MA + n + 1, 1, u)
                    if tail and u == 0:
                        head_lo(GLA, HA - 1, bass.ds(4 * HA - 4, 4))
                if tail:
                    for b in range(4):
                        dve.wait_ge(st_out[b], 16 * 2 * HA)
                    dve.wait_ge(ps_out, 16 * HA)
                slab_read(dve, M_MA + n, 1)
                slab_done(dve, M_MA + n + 1, 0)
                dve.tensor_tensor(m_sb[:, bass.ds(2 * n, 2), :], acc[0][:, :, 0:T], gate, ALU.mult)\
                   .then_inc(acc_free[0], 1)

            def merged_to_lo(c):
                at = slice(4 * c, 4 * c + 4)
                dve.wait_ge(merged_hi, c + 1)
                dve.tensor_tensor(a_lo[:, at, :], m_sb[:, at, :], a_hi[:, at, :].bitcast(F32), ALU.subtract)\
                   .then_inc(merged_ready, 1)

            def merge_b(n, tail, last=False):
                for u in range(UNITS):
                    split(M_MB + n + 1, 0, u)
                    if tail:
                        hgrn_tail(HPAIRS - 1, u)
                if tail:
                    hgrn_tail(HPAIRS - 1, 4)
                    head_gate(HG, HPAIRS - 1)
                    keep_own_decays()
                for u in range(UNITS):
                    split(M_MB + n + 1, 1, u)
                    if tail and u == 0:
                        head_lo(HG, HPAIRS - 1, bass.ds(2 * HPAIRS - 2, 2))
                    if tail and u >= 2:
                        hgrn_states(HPAIRS - 1, 3 - u)
                    if last and u < UNITS - 1:
                        merged_to_lo(u)
                slab_read(dve, M_MB + n, 1)
                slab_done(dve, M_MB + n + 1, 0)
                dve.tensor_tensor(gate, acc[0][:, :, 0:T], gate, ALU.mult).then_inc(acc_free[0], 1)
                slab_read(dve, M_MB + n + 1, 0)
                tile = m_sb[:, bass.ds(2 * n, 2), :]
                dve.tensor_tensor(tile, tile, gate, ALU.add).then_inc(merged, 1)

            def add_squares(index, clears):
                dve.wait_ge(res_sq, index + 1)
                dve.wait_ge(sq_summed, index + clears)
                dve.tensor_tensor(sq_sum, sq_sum, sq_new, ALU.add).then_inc(sq_summed, 1)

            def out_end(m, par, index):
                slab_done(dve, m, par)
                dve.tensor_tensor(m_sb[:, bass.ds(2 * index, 2), :], acc[par][:, :, 0:T],
                                  x_res[:, bass.ds(2 * index, 2), :], ALU.add).then_inc(acc_free[par], 1)
                dve.wait_ge(res_hi, index + 1)
                for j in range(2):
                    at = bass.ds(2 * index + j, 1)
                    ins = dve.scalar_tensor_tensor(out=b_lo[:, at, :], in0=m_sb[:, at, :],
                                                   scalar=vec[:, bass.ds(2 * index + (V_MLP + j), 1)],
                                                   in1=b_hi[:, at, :].bitcast(F32), op0=ALU.mult,
                                                   op1=ALU.subtract)
                ins.then_inc(res_ready, 1)
                add_squares(index, 1)

            def up_end(m, par, index, c):
                slab_done(dve, m, par)
                dve.scalar_tensor_tensor(out=hid_t, in0=acc[par][:, :, 0:T], scalar=0.0,
                                         in1=norm[:, 0:1, :].to_broadcast([P, 2, T]), op0=ALU.max,
                                         op1=ALU.mult).then_inc(acc_free[par], 1)
                dve.wait_ge(hid_hi, c * NS2 + index + 1)
                at = bass.ds(2 * index, 2)
                dve.tensor_tensor(a_lo[:, at, :], hid_f, a_hi[:, at, :].bitcast(F32), ALU.subtract)\
                   .then_inc(hid_ready, 1)

            def up_pair(n, c, first=False):
                m = M_UP + M_Q * c + n
                for u in range(UNITS):
                    split(m + 1, 0, u)
                    if first and u == 2:
                        stream_norm(LATE + 1, HA + HPAIRS + 2)
                        dve.memset(sq_sum, 0.0).then_inc(sq_summed, 1)
                up_end(m, 1, 2 * n, c)
                for u in range(UNITS):
                    split(m + 1, 1, u)
                up_end(m + 1, 0, 2 * n + 1, c)

            def up(c):
                with dve.Fori(0, NS2 // 2) as n:
                    up_pair(n, c)

            def down_end(m, par, tile):
                slab_done(dve, m, par)
                dve.wait_ge(acc_free[par], m)
                at = m_sb[:, bass.ds(tile, 2), :]
                dve.tensor_tensor(at, at, acc[par][:, :, 0:T], ALU.add).then_inc(acc_free[par], 1)

            def final_gain(tile):
                for j in range(2):
                    at = m_sb[:, bass.ds(tile + j, 1), :]
                    ins = dve.tensor_scalar(at, at, vec[:, bass.ds(tile + (V_FIN + j), 1)], 1.0, ALU.mult, ALU.mult)
                return ins

            def down(n, c, last, end):
                m = M_DOWN + M_Q * c + n
                for u in range(UNITS):
                    split(m + 1, 0, u)
                down_end(m, 1, 4 * n)
                if last:
                    add_squares(2 * n + NS2, 2)
                    final_gain(4 * n)
                for u in range(UNITS):
                    if not end:
                        split(m + 1, 1, u)
                down_end(m + 1, 0, 4 * n + 2)
                if last:
                    add_squares(2 * n + (NS2 + 1), 2)
                    final_gain(4 * n + 2)

            def stream_norm(count, guesses):
                dve.wait_ge(full[0], count)
                mean(norm[:, 0, :], 0, D).then_inc(free[0], 1)
                refine(norm[:, 0, :], guess, guesses)

            dve.memset(sc, 0.0)

            def mix_gain(c):
                for i in range(4 * c, 4 * c + 4):
                    dve.tensor_scalar(m_sb[:, i, :], m_sb[:, i, :], vec[:, V_MIX + i:V_MIX + i + 1], 1.0,
                                      ALU.mult, ALU.mult)

            dve.wait_ge(vec_there, 16)
            first, second, most = vec[:, V_LB0:V_LB0 + KT], vec[:, V_LB1:V_LB1 + KT], soft[:, 2, :]
            me.link(dve.tensor_tensor(most, first, second, ALU.max))
            dve.tensor_tensor(soft[:, 0, :], first, most, ALU.subtract)
            dve.tensor_tensor(soft[:, 1, :], second, most, ALU.subtract).then_inc(lb_max, 1)
            dve.wait_ge(sq_in_made, 1)
            mix_gain(0)
            for c in range(1, 4):
                dve.wait_ge(sq_in_made, c + 1)
                wait_from(dve, sq_in_added, c - 1)
                dve.tensor_tensor(sq_in[0], sq_in[0], sq_in[(0, 1, 2, 1)[c]], ALU.add).then_inc(sq_in_added, 1)
            dve.wait_ge(sq_in_added, 3)
            dve.tensor_tensor(sq_in[0][:, 0:2, :], sq_in[0][:, 0:2, :], sq_in[0][:, 2:4, :], ALU.add)\
               .then_inc(sq_in_added, 1)
            mix_gain(1)
            dve.wait_ge(full[0], 1)
            mean(norm[:, 0, :], 0, D).then_inc(free[0], 1)
            split(0, 0, 0)
            mix_gain(2)
            refine(norm[:, 0, :], guess, 1)
            for c in range(UNITS):
                tiles, at = m_sb[:, 4 * c:4 * c + 4, :], slice(4 * c, 4 * c + 4)
                dve.tensor_tensor(tiles, tiles, norm[:, 0:1, :].to_broadcast([P, 4, T]), ALU.mult)\
                   .then_inc(h_made, 1)
                if c < 2:
                    split(0, 0, c + 1)
                else:
                    split(0, 1, c - 2)
                dve.wait_ge(h_hi, c + 1)
                dve.tensor_tensor(a_lo[:, at, :], m_sb[:, at, :], a_hi[:, at, :].bitcast(F32), ALU.subtract)\
                   .then_inc(h_ready, 1)
                if c == 1:
                    mix_gain(3)
                    split(0, 0, 3)
            split(0, 1, 2)
            split(0, 1, 3)
            dve.wait_ge(consts_in, 16 * 3)
            dve.tensor_copy(masks[:], masks_f)
            gla_head(0, False)
            dve.wait_ge(lb_exp, 1)
            me.link(dve.tensor_tensor(most, soft[:, 0, :], soft[:, 1, :], ALU.add))
            me.link(dve.reciprocal(most, most))
            me.link(dve.tensor_tensor(lb[:], soft[:, 0, :], most, ALU.mult))
            me.link(dve.tensor_scalar(one_lb[:], lb[:], -1.0, 1.0, ALU.mult, ALU.add))
            with me.loop(1, HA, LEVELS - 1 + 5) as h:
                gla_head(h, True)
            merge_a(0, True)
            with dve.Fori(1, NS2) as n:
                merge_a(n, False)
            hgrn_pair(0, False)
            with me.loop(1, HPAIRS, LEVELS - 1 + 7) as n:
                hgrn_pair(n, True)
            merge_b(0, True)
            with dve.Fori(1, NS2 - 1) as n:
                merge_b(n, False)
            merge_b(NS2 - 1, False, last=True)
            merged_to_lo(UNITS - 1)
            dve.memset(sq_sum, 0.0).then_inc(sq_summed, 1)
            dve.wait_ge(x_res_in, 16)
            with dve.Fori(0, NS2 // 2) as n:
                for u in range(UNITS):
                    split(M_OUT + n + 1, 0, u)
                out_end(M_OUT + n, 1, 2 * n)
                for u in range(UNITS):
                    split(M_OUT + n + 1, 1, u)
                out_end(M_OUT + n + 1, 0, 2 * n + 1)
            dve.sem_inc(hid_ready, 1)
            up_pair(0, 0, first=True)
            with dve.Fori(1, NS2 // 2) as n:
                up_pair(n, 0)
            with dve.Fori(0, NS2 // 2) as n:
                down(n, 0, False, False)
            with dve.Fori(1, QUARTERS - 1) as c:
                up(c)
                with dve.Fori(0, NS2 // 2) as n:
                    down(n, c, False, False)
            up(QUARTERS - 1)
            with dve.Fori(0, NS2 // 2 - 1) as n:
                down(n, QUARTERS - 1, True, False)
            down(NS2 // 2 - 1, QUARTERS - 1, True, True)
            stream_norm(LATE + 2, HA + HPAIRS + 3)
            dve.sem_inc(rstd_made, 1)
            for c in range(Y_DVE):
                tiles = m_sb[:, 2 * c:2 * c + 2, :]
                dve.tensor_tensor(tiles, tiles, norm[:, 0:1, :].to_broadcast([P, 2, T]), ALU.mult).then_inc(y_made, 1)


def _masks():
    import numpy as np

    s = np.arange(P)[:, None]
    out = [s == np.arange(P)[None, :]]
    for level in range(6):
        t = np.array([x for x in range(P) if x >> level & 1])[None, :]
        out.append((s >> (level + 1) == t >> (level + 1)) & (s >> level & 1 == 0))
    return np.concatenate(out, axis=1).astype(np.float32)


def kernel(**inputs):
    import numpy as np

    import concourse.bacc as bacc
    from concourse.bass_utils import run_bass_kernel_spmd

    a = {name: np.asarray(value) for name, value in inputs.items()}
    tokens = np.concatenate([a["x_prompt"].reshape(NPR, D), a["x_sample"].reshape(NSM, D)])
    rows = [a["norm_mix"], a["norm_mlp"], a["norm_final"], a["hg_lower_bound"], a["b_gate2"], a["gla_norm"],
            a["hg_norm"]]
    arrays = {
        "x_t": tokens.T,
        "state_gla": a["state_gla"][0],
        "state_hgrn": a["state_hgrn"][0],
        "vectors": np.concatenate([r.reshape(-1, P) for r in rows]).T,
        "w_in": a["w_in"][0],
        "w_gate2": a["w_gate2"][0],
        "w_branch_a": a["w_branch_a"][0],
        "w_branch_b": a["w_branch_b"][0],
        "w_out": a["w_out"][0],
        "w_up": a["w_up"][0],
        "w_down": a["w_down"][0],
        "ones_in": np.ones((P, P), np.float32),
        "eye_in": np.eye(P, dtype=np.float32),
        "own_in": np.tile(np.repeat(np.eye(SB, dtype=np.float32), SL, axis=0), (2, 1)),
        "masks_in": _masks(),
    }
    arrays = {f"{name}_dram": np.ascontiguousarray(value) for name, value in arrays.items()}
    outs = {"y_t": (D, T), "new_gla_prompt": (HA, DKA, DVA), "new_hgrn_prompt": (HB, P, P),
            "new_gla_sample": (SB, HA, DKA, DVA), "new_hgrn_sample": (SB, HB, P, P)}
    nc = bacc.Bacc("TRN2", target_bir_lowering=False, num_devices=1)
    args = [nc.dram_tensor(name, v.shape, mybir.dt.from_np(v.dtype), kind="ExternalInput").ap()
            for name, v in arrays.items()]
    args += [nc.dram_tensor(name, shape, F32, kind="ExternalOutput").ap() for name, shape in outs.items()]
    gated_merge_step(nc, *args)
    got = run_bass_kernel_spmd(nc, [arrays], core_ids=[0]).results[0]
    y = np.ascontiguousarray(got["y_t"].T)
    return (y[:NPR].reshape(1, NPR, D), y[NPR:].reshape(SB, SL, D),
            got["new_gla_prompt"].reshape(1, 1, HA, DKA, DVA), got["new_hgrn_prompt"].reshape(1, 1, HB, P, P),
            got["new_gla_sample"].reshape(1, SB, HA, DKA, DVA), got["new_hgrn_sample"].reshape(1, SB, HB, P, P))
```
